# Optimizing a Trainium2 kernel written in Bass

```python
import jax, jax.numpy as jnp
from jax import lax
import numpy as np
import math

D_MODEL = 1024
BATCH = 1
SEQ = 256
DEPTH = 2

N_MIXERS = 2
N_A_LAYERS = (DEPTH + 1) // 2
N_B_LAYERS = DEPTH // 2
EPS = 1e-6

D_FF = ((8 * D_MODEL // 3 + 127) // 128) * 128

A_DK = 128
A_DV = 128
A_HEADS = D_MODEL // A_DK
A_CONV = 4
A_CHUNK = 64

B_HD = 64
B_HEADS = D_MODEL // B_HD
B_KV_HEADS = 4
B_WINDOW = 128
B_BLOCK = 128


def rmsnorm(x, w):
    xf = x.astype(jnp.float32)
    y = xf * lax.rsqrt(jnp.mean(xf * xf, axis=-1, keepdims=True) + EPS) * w.astype(jnp.float32)
    return y.astype(x.dtype)

def l2norm(x):
    xf = x.astype(jnp.float32)
    return xf * lax.rsqrt(jnp.sum(xf * xf, axis=-1, keepdims=True) + EPS)

def swiglu(h, w_gu, w_down):
    gate, up = jnp.split(h @ w_gu, 2, axis=-1)
    return (jax.nn.silu(gate) * up) @ w_down

def causal_depthwise_conv(x, w):
    C = x.shape[-1]
    return lax.conv_general_dilated(
        x, w[:, None, :].astype(x.dtype), window_strides=(1,), padding=[(A_CONV - 1, 0)],
        dimension_numbers=("NWC", "WIO", "NWC"), feature_group_count=C)

def gated_delta_rule_chunked(q, k, v, g, beta):
    Bsz, T, H, DK = q.shape
    DV = v.shape[-1]
    C = A_CHUNK
    N = T // C
    f32 = jnp.float32

    def chunk(t):
        return t.astype(f32).reshape(Bsz, N, C, H, -1).transpose(0, 3, 1, 2, 4)

    q, k, v = chunk(q), chunk(k), chunk(v)
    g = g.astype(f32).reshape(Bsz, N, C, H).transpose(0, 3, 1, 2)
    beta = beta.astype(f32).reshape(Bsz, N, C, H).transpose(0, 3, 1, 2)
    g = jnp.cumsum(g, axis=-1)

    idx = jnp.arange(C)
    lower_incl = idx[:, None] >= idx[None, :]
    strict = idx[:, None] > idx[None, :]
    decay = jnp.exp(jnp.where(lower_incl, g[..., :, None] - g[..., None, :], -jnp.inf))

    kb = k * beta[..., None]
    L = jnp.where(strict, jnp.einsum("bhnid,bhnjd->bhnij", kb, k) * decay, 0.0)
    rhs = jnp.concatenate([v * beta[..., None], kb * jnp.exp(g)[..., None]], axis=-1)
    sol = lax.linalg.triangular_solve(L, rhs, left_side=True, lower=True,
                                      transpose_a=False, conjugate_a=False, unit_diagonal=True)
    u, w = sol[..., :DV], sol[..., DV:]

    a_qk = jnp.einsum("bhnid,bhnjd->bhnij", q, k) * decay
    q_dec = q * jnp.exp(g)[..., None]
    k_dec = k * jnp.exp(g[..., -1:] - g)[..., None]
    g_last = jnp.exp(g[..., -1])

    xs = (jnp.moveaxis(q_dec, 2, 0), jnp.moveaxis(k_dec, 2, 0), jnp.moveaxis(u, 2, 0),
          jnp.moveaxis(w, 2, 0), jnp.moveaxis(a_qk, 2, 0), jnp.moveaxis(g_last, 2, 0))

    def step(S, inp):
        qd, kd, u_c, w_c, a_c, gl = inp
        v_new = u_c - jnp.einsum("bhck,bhkv->bhcv", w_c, S)
        o = jnp.einsum("bhck,bhkv->bhcv", qd, S) + jnp.einsum("bhij,bhjv->bhiv", a_c, v_new)
        S = S * gl[..., None, None] + jnp.einsum("bhck,bhcv->bhkv", kd, v_new)
        return S, o

    S0 = jnp.zeros((Bsz, H, DK, DV), f32)
    _, o = lax.scan(step, S0, xs)
    return o.transpose(1, 0, 3, 2, 4).reshape(Bsz, T, H, DV)

def mixer_gated_deltanet(h, w_in, w_conv, A_log, dt_bias, out_norm, w_out):
    Bsz, T, _ = h.shape
    HK = A_HEADS * A_DK
    HV = A_HEADS * A_DV
    proj = h @ w_in
    qkv = proj[..., :2 * HK + HV]
    z = proj[..., 2 * HK + HV:2 * HK + 2 * HV]
    b = proj[..., 2 * HK + 2 * HV:2 * HK + 2 * HV + A_HEADS]
    a = proj[..., 2 * HK + 2 * HV + A_HEADS:]
    qkv = jax.nn.silu(causal_depthwise_conv(qkv, w_conv))
    q = l2norm(qkv[..., :HK].reshape(Bsz, T, A_HEADS, A_DK)) * (A_DK ** -0.5)
    k = l2norm(qkv[..., HK:2 * HK].reshape(Bsz, T, A_HEADS, A_DK))
    v = qkv[..., 2 * HK:].reshape(Bsz, T, A_HEADS, A_DV)
    beta = jax.nn.sigmoid(b.astype(jnp.float32))
    g = -jnp.exp(A_log.astype(jnp.float32)) * jax.nn.softplus(a.astype(jnp.float32) + dt_bias.astype(jnp.float32))
    o = gated_delta_rule_chunked(q, k, v, g, beta)
    zf = z.reshape(Bsz, T, A_HEADS, A_DV).astype(jnp.float32)
    o = rmsnorm(o, out_norm) * jax.nn.silu(zf)
    return o.reshape(Bsz, T, HV).astype(h.dtype) @ w_out

def mixer_sliding_window_sinks(h, w_in, b_in, sinks, w_out, b_out):
    Bsz, T, _ = h.shape
    G = B_HEADS // B_KV_HEADS
    NB = T // B_BLOCK
    HQ = B_HEADS * B_HD
    HKV = B_KV_HEADS * B_HD
    proj = h @ w_in + b_in
    q = proj[..., :HQ].reshape(Bsz, NB, B_BLOCK, B_KV_HEADS, G, B_HD)
    k = proj[..., HQ:HQ + HKV].reshape(Bsz, NB, B_BLOCK, B_KV_HEADS, B_HD)
    v = proj[..., HQ + HKV:].reshape(Bsz, NB, B_BLOCK, B_KV_HEADS, B_HD)

    def with_prev(t):
        prev = jnp.concatenate([jnp.zeros_like(t[:, :1]), t[:, :-1]], axis=1)
        return jnp.concatenate([prev, t], axis=2)

    kk, vv = with_prev(k), with_prev(v)
    s = jnp.einsum("bnqhgd,bnkhd->bnhgqk", q, kk).astype(jnp.float32) * (B_HD ** -0.5)
    qi = jnp.arange(B_BLOCK)[:, None]
    kj = jnp.arange(2 * B_BLOCK)[None, :]
    rel = qi + B_BLOCK - kj
    band = (rel >= 0) & (rel < B_WINDOW)
    blk = jnp.arange(NB)[:, None, None]
    valid = band[None] & ((blk > 0) | (kj >= B_BLOCK)[None])
    s = jnp.where(valid[None, :, None, None], s, -jnp.inf)
    sink = jnp.broadcast_to(sinks.astype(jnp.float32).reshape(B_KV_HEADS, G)[None, None, :, :, None, None],
                            s.shape[:-1] + (1,))
    p = jax.nn.softmax(jnp.concatenate([s, sink], axis=-1), axis=-1)[..., :-1]
    o = jnp.einsum("bnhgqk,bnkhd->bnqhgd", p.astype(vv.dtype), vv)
    return o.reshape(Bsz, T, HQ) @ w_out + b_out

def first_inputs(seed: int = 0) -> dict:
    key = jax.random.key(seed)
    ks = iter(jax.random.split(key, 32))
    f32 = jnp.float32
    nrm = lambda shape, scale: jax.random.normal(next(ks), shape, f32) * scale
    gain = lambda shape: 1.0 + 0.02 * jax.random.normal(next(ks), shape, f32)
    D = D_MODEL
    a_in_cols = 2 * A_HEADS * A_DK + 2 * A_HEADS * A_DV + 2 * A_HEADS
    b_in_cols = (B_HEADS + 2 * B_KV_HEADS) * B_HD
    dt = jnp.exp(jax.random.uniform(next(ks), (N_A_LAYERS, A_HEADS), f32, np.log(1e-3), np.log(1e-1)))
    return {
        "x": jax.random.normal(next(ks), (BATCH, SEQ, D), f32),
        "ffn1_norm": gain((DEPTH, D)),
        "ffn1_w_gu": nrm((DEPTH, D, 2 * D_FF), D ** -0.5),
        "ffn1_w_down": nrm((DEPTH, D_FF, D), D_FF ** -0.5),
        "mix_norm": gain((DEPTH, D)),
        "ffn2_norm": gain((DEPTH, D)),
        "ffn2_w_gu": nrm((DEPTH, D, 2 * D_FF), D ** -0.5),
        "ffn2_w_down": nrm((DEPTH, D_FF, D), D_FF ** -0.5),
        "a_w_in": nrm((N_A_LAYERS, D, a_in_cols), D ** -0.5),
        "a_w_conv": nrm((N_A_LAYERS, A_CONV, 2 * A_HEADS * A_DK + A_HEADS * A_DV), A_CONV ** -0.5),
        "a_A_log": jnp.log(jax.random.uniform(next(ks), (N_A_LAYERS, A_HEADS), f32, 1.0, 16.0)),
        "a_dt_bias": dt + jnp.log(-jnp.expm1(-dt)),
        "a_out_norm": gain((N_A_LAYERS, A_DV)),
        "a_w_out": nrm((N_A_LAYERS, A_HEADS * A_DV, D), (A_HEADS * A_DV) ** -0.5),
        "b_w_in": nrm((N_B_LAYERS, D, b_in_cols), D ** -0.5),
        "b_b_in": nrm((N_B_LAYERS, b_in_cols), 0.02),
        "b_sinks": nrm((N_B_LAYERS, B_HEADS), 1.0),
        "b_w_out": nrm((N_B_LAYERS, B_HEADS * B_HD, D), (B_HEADS * B_HD) ** -0.5),
        "b_b_out": nrm((N_B_LAYERS, D), 0.02),
        "final_norm": gain((D,)),
    }

def first_block(x, ffn1_norm, ffn1_w_gu, ffn1_w_down, mix_norm, ffn2_norm, ffn2_w_gu, ffn2_w_down,
              a_w_in, a_w_conv, a_A_log, a_dt_bias, a_out_norm, a_w_out,
              b_w_in, b_b_in, b_sinks, b_w_out, b_b_out, final_norm):
    for layer in range(DEPTH):
        x = x + 0.5 * swiglu(rmsnorm(x, ffn1_norm[layer]), ffn1_w_gu[layer], ffn1_w_down[layer])
        h = rmsnorm(x, mix_norm[layer])
        j = layer // N_MIXERS
        if layer % N_MIXERS == 0:
            y = mixer_gated_deltanet(h, a_w_in[j], a_w_conv[j], a_A_log[j], a_dt_bias[j],
                                     a_out_norm[j], a_w_out[j])
        else:
            y = mixer_sliding_window_sinks(h, b_w_in[j], b_b_in[j], b_sinks[j], b_w_out[j], b_b_out[j])
        x = x + y
        x = x + 0.5 * swiglu(rmsnorm(x, ffn2_norm[layer]), ffn2_w_gu[layer], ffn2_w_down[layer])
    return rmsnorm(x, final_norm)


DEPTH_2 = 1

N_META = 16
CHUNK = 128
META_PAD = (-N_META) % CHUNK
RET_HEADS = 8
RET_DK = 64
RET_DV = 128
RET_QK_W = RET_HEADS * RET_DK
RET_V_W = RET_HEADS * RET_DV
MLA_HEADS = 8
MLA_Q_RANK = 384
MLA_KV_RANK = 256
MLA_NOPE = 64
MLA_ROPE = 32
MLA_DV = 64
MLA_QK = MLA_NOPE + MLA_ROPE
D_FF_2 = ((-(-8 * D_MODEL // 3) + 255) // 256) * 256
ROPE_BASE = 10000.0
RMS_EPS = 1e-6
GN_EPS = 1e-5

SPLIT_SIZES = (RET_QK_W, RET_QK_W, RET_V_W, RET_V_W, MLA_Q_RANK, MLA_KV_RANK, MLA_ROPE, D_MODEL, D_MODEL)
SPLIT_IDX = tuple(int(s) for s in np.cumsum(SPLIT_SIZES)[:-1])
D_IN = int(sum(SPLIT_SIZES))


def _rmsnorm(x, w):
    xf = x.astype(jnp.float32)
    y = xf * lax.rsqrt(jnp.mean(xf * xf, axis=-1, keepdims=True) + RMS_EPS)
    return (y * w.astype(jnp.float32)).astype(x.dtype)

def _rope_tables(pos, dim):
    half = dim // 2
    inv = ROPE_BASE ** (-jnp.arange(half, dtype=jnp.float32) / half)
    ang = pos.astype(jnp.float32)[:, None] * inv[None, :]
    return jnp.cos(ang), jnp.sin(ang)

def _apply_rope(x, cos, sin):
    half = x.shape[-1] // 2
    xf = x.astype(jnp.float32)
    x1, x2 = xf[..., :half], xf[..., half:]
    return jnp.concatenate([x1 * cos - x2 * sin, x1 * sin + x2 * cos], axis=-1).astype(x.dtype)

def _retention_dir(q, k, v, log_gamma, inclusive):
    B, Lp, H, dk = q.shape
    dv = v.shape[-1]
    n = Lp // CHUNK
    qc = q.reshape(B, n, CHUNK, H, dk)
    kc = k.reshape(B, n, CHUNK, H, dk)
    vc = v.reshape(B, n, CHUNK, H, dv)
    lg = log_gamma.astype(jnp.float32)
    idx = jnp.arange(CHUNK, dtype=jnp.float32)
    rel = idx[:, None] - idx[None, :]
    mask = rel >= 0 if inclusive else rel > 0
    dmask = jnp.exp(jnp.where(mask[None], lg[:, None, None] * rel[None], -jnp.inf)).astype(q.dtype)
    scores = jnp.einsum('bnihd,bnjhd->bnhij', qc, kc) * dmask
    inner = jnp.einsum('bnhij,bnjhe->bnihe', scores, vc)
    w_k = jnp.exp(lg[None, :] * (CHUNK - 1 - idx)[:, None]).astype(q.dtype)
    incr = jnp.einsum('bnjhd,jh,bnjhe->nbhde', kc, w_k, vc)
    g_chunk = jnp.exp(lg * CHUNK).astype(incr.dtype)[None, :, None, None]

    def step(state, u):
        return g_chunk * state + u, state

    state0 = jnp.zeros((B, H, dk, dv), incr.dtype)
    _, states_prev = lax.scan(step, state0, incr)
    w_q = jnp.exp(lg[None, :] * (idx + 1.0)[:, None]).astype(q.dtype)
    cross = jnp.einsum('bnihd,ih,nbhde->bnihe', qc, w_q, states_prev)
    return (inner + cross).reshape(B, Lp, H, dv)

def _bidir_retention(q, k, v, decay_f, decay_b):
    lg_f = -jnp.exp(decay_f.astype(jnp.float32))
    lg_b = -jnp.exp(decay_b.astype(jnp.float32))
    pad = ((0, 0), (META_PAD, 0), (0, 0), (0, 0))
    qp, kp, vp = jnp.pad(q, pad), jnp.pad(k, pad), jnp.pad(v, pad)
    fwd = _retention_dir(qp, kp, vp, lg_f, True)
    bwd = jnp.flip(_retention_dir(jnp.flip(qp, 1), jnp.flip(kp, 1), jnp.flip(vp, 1), lg_b, False), 1)
    return (fwd + bwd)[:, META_PAD:]

def _head_group_norm(y, w):
    B, L, H, dv = y.shape
    yf = y.astype(jnp.float32)
    mu = jnp.mean(yf, axis=-1, keepdims=True)
    var = jnp.mean(jnp.square(yf - mu), axis=-1, keepdims=True)
    yn = ((yf - mu) * lax.rsqrt(var + GN_EPS)).reshape(B, L, H * dv)
    return (yn * w.astype(jnp.float32)).astype(y.dtype)

def _mla_attention(q_nope, q_rope, k_nope, k_rope, v):
    B, L, H, _ = q_nope.shape
    Lp = L + META_PAD
    nb = Lp // CHUNK
    scale = MLA_QK ** -0.5

    def to_blocks(t):
        t = jnp.pad(t, ((0, 0), (META_PAD, 0), (0, 0), (0, 0)))
        return t.reshape(B, nb, CHUNK, H, t.shape[-1]).swapaxes(0, 1)

    def attend(qb):
        qn, qr = qb
        s = jnp.einsum('bqhd,bkhd->bhqk', qn, k_nope) + jnp.einsum('bqhr,bkr->bhqk', qr, k_rope)
        p = jax.nn.softmax(s.astype(jnp.float32) * scale, axis=-1).astype(v.dtype)
        return jnp.einsum('bhqk,bkhd->bqhd', p, v)

    out = lax.map(attend, (to_blocks(q_nope), to_blocks(q_rope)))
    return out.swapaxes(0, 1).reshape(B, Lp, H, MLA_DV)[:, META_PAD:]

def _mixer(u, w_in, decay_f, decay_b, gn_w, w_ret_out, q_norm_w, w_uq, kv_norm_w, w_uk, w_uv,
           w_mla_out, w_o, ret_cos, ret_sin, mla_cos, mla_sin):
    B, L, _ = u.shape
    proj = u @ w_in
    rq, rk, rv, rg, a_cq, a_ckv, a_kr, a_gret, a_gmla = jnp.split(proj, SPLIT_IDX, axis=-1)

    rq = _apply_rope(rq.reshape(B, L, RET_HEADS, RET_DK), ret_cos[:, None, :], ret_sin[:, None, :])
    rk = _apply_rope(rk.reshape(B, L, RET_HEADS, RET_DK), ret_cos[:, None, :], ret_sin[:, None, :]) * (RET_DK ** -0.5)
    rv = rv.reshape(B, L, RET_HEADS, RET_DV)
    y_ret = _head_group_norm(_bidir_retention(rq, rk, rv, decay_f, decay_b), gn_w)
    y_ret = (jax.nn.silu(rg) * y_ret) @ w_ret_out

    c_q = _rmsnorm(a_cq, q_norm_w)
    q = (c_q @ w_uq).reshape(B, L, MLA_HEADS, MLA_QK)
    q_nope = q[..., :MLA_NOPE]
    q_rope = _apply_rope(q[..., MLA_NOPE:], mla_cos[:, None, :], mla_sin[:, None, :])
    c_kv = _rmsnorm(a_ckv, kv_norm_w)
    k_nope = (c_kv @ w_uk).reshape(B, L, MLA_HEADS, MLA_NOPE)
    v = (c_kv @ w_uv).reshape(B, L, MLA_HEADS, MLA_DV)
    k_rope = _apply_rope(a_kr, mla_cos, mla_sin)
    y_mla = _mla_attention(q_nope, q_rope, k_nope, k_rope, v).reshape(B, L, MLA_HEADS * MLA_DV) @ w_mla_out

    merged = jax.nn.sigmoid(a_gret) * y_ret + jax.nn.sigmoid(a_gmla) * y_mla
    return merged @ w_o

def _swiglu(u, w_gate, w_up, w_down):
    return (jax.nn.silu(u @ w_gate) * (u @ w_up)) @ w_down

def second_inputs(seed: int = 0) -> dict:
    key = jax.random.key(seed)
    ks = jax.random.split(key, 24)
    f32 = jnp.float32

    def nrm(k, shape, fan_in):
        return jax.random.normal(k, shape, f32) * (fan_in ** -0.5)

    def gain(k, shape):
        return 1.0 + 0.02 * jax.random.normal(k, shape, f32)

    h_idx = jnp.arange(RET_HEADS, dtype=f32)
    gamma = 1.0 - 2.0 ** (-5.0 - h_idx)
    decay_base = jnp.log(-jnp.log(gamma))
    return {
        'x': jax.random.normal(ks[0], (BATCH, SEQ, D_MODEL), f32),
        'meta_tokens': jax.random.normal(ks[1], (N_META, D_MODEL), f32),
        'norm_mix_w': gain(ks[2], (DEPTH_2, D_MODEL)),
        'w_in': nrm(ks[3], (DEPTH_2, D_MODEL, D_IN), D_MODEL),
        'ret_decay_fwd': decay_base[None] + 0.05 * jax.random.normal(ks[4], (DEPTH_2, RET_HEADS), f32),
        'ret_decay_bwd': decay_base[None] + 0.05 * jax.random.normal(ks[5], (DEPTH_2, RET_HEADS), f32),
        'ret_gn_w': gain(ks[6], (DEPTH_2, RET_V_W)),
        'w_ret_out': nrm(ks[7], (DEPTH_2, RET_V_W, D_MODEL), RET_V_W),
        'mla_q_norm_w': gain(ks[8], (DEPTH_2, MLA_Q_RANK)),
        'w_uq': nrm(ks[9], (DEPTH_2, MLA_Q_RANK, MLA_HEADS * MLA_QK), MLA_Q_RANK),
        'mla_kv_norm_w': gain(ks[10], (DEPTH_2, MLA_KV_RANK)),
        'w_uk': nrm(ks[11], (DEPTH_2, MLA_KV_RANK, MLA_HEADS * MLA_NOPE), MLA_KV_RANK),
        'w_uv': nrm(ks[12], (DEPTH_2, MLA_KV_RANK, MLA_HEADS * MLA_DV), MLA_KV_RANK),
        'w_mla_out': nrm(ks[13], (DEPTH_2, MLA_HEADS * MLA_DV, D_MODEL), MLA_HEADS * MLA_DV),
        'w_o': nrm(ks[14], (DEPTH_2, D_MODEL, D_MODEL), D_MODEL),
        'norm_ffn_w': gain(ks[15], (DEPTH_2, D_MODEL)),
        'w_ffn_gate': nrm(ks[16], (DEPTH_2, D_MODEL, D_FF_2), D_MODEL),
        'w_ffn_up': nrm(ks[17], (DEPTH_2, D_MODEL, D_FF_2), D_MODEL),
        'w_ffn_down': nrm(ks[18], (DEPTH_2, D_FF_2, D_MODEL), D_FF_2),
        'norm_final_w': gain(ks[19], (D_MODEL,)),
    }

def second_block(x, meta_tokens, norm_mix_w, w_in, ret_decay_fwd, ret_decay_bwd, ret_gn_w, w_ret_out,
              mla_q_norm_w, w_uq, mla_kv_norm_w, w_uk, w_uv, w_mla_out, w_o, norm_ffn_w,
              w_ffn_gate, w_ffn_up, w_ffn_down, norm_final_w):
    B, S, D = x.shape
    L = S + N_META
    meta = jnp.broadcast_to(meta_tokens.astype(x.dtype)[None], (B, N_META, D))
    h = jnp.concatenate([meta, x], axis=1)
    pos = jnp.arange(L)
    ret_cos, ret_sin = _rope_tables(pos, RET_DK)
    mla_cos, mla_sin = _rope_tables(pos, MLA_ROPE)
    for l in range(DEPTH_2):
        h = h + _mixer(_rmsnorm(h, norm_mix_w[l]), w_in[l], ret_decay_fwd[l], ret_decay_bwd[l], ret_gn_w[l],
                       w_ret_out[l], mla_q_norm_w[l], w_uq[l], mla_kv_norm_w[l], w_uk[l], w_uv[l],
                       w_mla_out[l], w_o[l], ret_cos, ret_sin, mla_cos, mla_sin)
        h = h + _swiglu(_rmsnorm(h, norm_ffn_w[l]), w_ffn_gate[l], w_ffn_up[l], w_ffn_down[l])
    h = _rmsnorm(h, norm_final_w)
    return h[:, N_META:]


def setup_inputs(seed=0):
    out = dict(first_inputs(seed))
    for name, value in second_inputs(seed + 1).items():
        if name != "x":
            out[name + "_2"] = value
    return out


def reference(
    x, ffn1_norm, ffn1_w_gu, ffn1_w_down, mix_norm, ffn2_norm, ffn2_w_gu, ffn2_w_down, a_w_in,
    a_w_conv, a_A_log, a_dt_bias, a_out_norm, a_w_out, b_w_in, b_b_in, b_sinks, b_w_out,
    b_b_out, final_norm, meta_tokens_2, norm_mix_w_2, w_in_2, ret_decay_fwd_2, ret_decay_bwd_2,
    ret_gn_w_2, w_ret_out_2, mla_q_norm_w_2, w_uq_2, mla_kv_norm_w_2, w_uk_2, w_uv_2,
    w_mla_out_2, w_o_2, norm_ffn_w_2, w_ffn_gate_2, w_ffn_up_2, w_ffn_down_2, norm_final_w_2,
):
    x = first_block(
        x, ffn1_norm, ffn1_w_gu, ffn1_w_down, mix_norm, ffn2_norm, ffn2_w_gu, ffn2_w_down,
        a_w_in, a_w_conv, a_A_log, a_dt_bias, a_out_norm, a_w_out, b_w_in, b_b_in, b_sinks,
        b_w_out, b_b_out, final_norm,
    )
    return second_block(
        x, meta_tokens_2, norm_mix_w_2, w_in_2, ret_decay_fwd_2, ret_decay_bwd_2, ret_gn_w_2,
        w_ret_out_2, mla_q_norm_w_2, w_uq_2, mla_kv_norm_w_2, w_uk_2, w_uv_2, w_mla_out_2,
        w_o_2, norm_ffn_w_2, w_ffn_gate_2, w_ffn_up_2, w_ffn_down_2, norm_final_w_2,
    )


_drawn_inputs = setup_inputs


def setup_inputs(seed=0):
    import zlib

    import numpy as np

    out = dict(_drawn_inputs(seed))
    spreads = {}
    factors = {'ffn1_norm': 3.349,
     'ffn2_norm': 4.405,
     'a_out_norm': 4.481,
     'b_sinks': 2.785,
     'norm_mix_w_2': 3.897,
     'ret_gn_w_2': 8.0,
     'mla_q_norm_w_2': 8.0,
     'mla_kv_norm_w_2': 8.0,
     'norm_ffn_w_2': 13.318,
     'b_b_in': 4.777,
     'b_b_out': 4.677}
    for name, (base, spread) in spreads.items():
        noise = np.random.default_rng([zlib.crc32(name.encode()), seed]).standard_normal(out[name].shape)
        drawn = base * np.exp(spread * noise) if base else spread * noise
        out[name] = __import__('jax').numpy.asarray(drawn.astype(out[name].dtype))
    for name, factor in factors.items():
        out[name] = (out[name] * factor).astype(out[name].dtype)
    return out
```

```python
from contextlib import ExitStack

import numpy as np
import concourse.bass as bass
from concourse import mybir

F32 = mybir.dt.float32
R32 = mybir.dt.float32r
ALU = mybir.AluOpType
ACT = mybir.ActivationFunctionType
AX = mybir.AxisListType

P = 128
D = 1024
KB = D // P
SEQ = 256
META = 16
TOK = SEQ + META
FF = 2816
HB = FF // P
UNITS = HB // 2
EPS = 1e-6
SLOTS = 4
WIDE = 256
NEG = -1.0e30

AH = 8
A_QKV = 3 * AH * P
A_IN = A_QKV + AH * P + 2 * AH
BH, BKV, BD = 16, 4, 64
RH, RDK, RDV = 8, 64, 128
MH, NOPE, ROPE, MDV = 8, 64, 32, 64
MQK = NOPE + ROPE
Q_RANK, KV_RANK = 384, 256
GN_EPS = 1e-5
TILES = [(0, 128), (128, 128), (256, 16)]


def slots_of_in(name, cols, row_blocks=KB, wide=WIDE):
    return [(name, 0, row_blocks, c, wide) for c in cols]


def out_slots(name, splits, row_block0=0):
    out = []
    for c in range(D // WIDE):
        k = row_block0
        for n in splits:
            out.append((name, k, n, c * WIDE, WIDE))
            k += n
    return out


FFN_SPLIT = [6, 6, 5, 5]

C_RQ, C_RK, C_RV, C_RG = 0, 512, 1024, 2048
C_CQ = 3072
C_CKV = C_CQ + Q_RANK
C_KR = C_CKV + KV_RANK
C_GRET = C_KR + ROPE
C_GMLA = C_GRET + D


def ffn_slots(gate, gate0, up, up0, down):
    s = []
    for u in range(UNITS):
        s += [(gate, 0, KB, gate0 + u * WIDE, WIDE), (up, 0, KB, up0 + u * WIDE, WIDE)]
    return s + out_slots(down, FFN_SPLIT)


def mixer_a_in_slots():
    s = [("a_w_in", 0, KB, A_IN - P, P)]
    return s + slots_of_in("a_w_in", range(0, A_QKV + AH * P, WIDE))


def mixer_r_in_slots():
    s = slots_of_in("w_in_2", list(range(C_RQ, C_RQ + 8 * WIDE, WIDE)))
    s += [("w_in_2", 0, KB, C_CQ, WIDE), ("w_in_2", 0, KB, C_CQ + WIDE, Q_RANK - WIDE), ("w_in_2", 0, KB, C_CKV, WIDE),
          ("w_in_2", 0, KB, C_KR, P)]
    s += slots_of_in("w_in_2", list(range(C_RQ + 8 * WIDE, C_CQ, WIDE)))
    return s + slots_of_in("w_in_2", list(range(C_GRET, C_GMLA + D, WIDE)))


def mla_slots():
    return [("w_uq_2", 0, 3, 0, 384), ("w_uq_2", 0, 3, 384, 384), ("w_uk_2", 0, 2, 0, 512), ("w_uv_2", 0, 2, 0, 512)]


B_ORDER = [4, 5, 0, 1, 2, 3]

STAGE_SLOTS = {
    "F0": lambda: ffn_slots("ffn1_w_gu_0", 0, "ffn1_w_gu_0", FF, "ffn1_w_down_0"),
    "A": lambda: mixer_a_in_slots() + out_slots("a_w_out", [8]),
    "F1": lambda: ffn_slots("ffn2_w_gu_0", 0, "ffn2_w_gu_0", FF, "ffn2_w_down_0"),
    "F2": lambda: ffn_slots("ffn1_w_gu_1", 0, "ffn1_w_gu_1", FF, "ffn1_w_down_1"),
    "B": lambda: slots_of_in("b_w_in", [WIDE * o for o in B_ORDER]) + out_slots("b_w_out", [8]),
    "F3": lambda: ffn_slots("ffn2_w_gu_1", 0, "ffn2_w_gu_1", FF, "ffn2_w_down_1"),
    "N": lambda: [],
    "R": lambda: (mixer_r_in_slots() + mla_slots() + out_slots("w_ret_out_2", [8])
                  + out_slots("w_mla_out_2", [4]) + out_slots("w_o_2", [8])),
    "F4": lambda: ffn_slots("w_ffn_gate_2", 0, "w_ffn_up_2", 0, "w_ffn_down_2"),
}
STAGES = ["F0", "A", "F1", "F2", "B", "F3", "N", "R", "F4"]

VEC_ROWS, VEC_N = {}, 0
for _name, _n in [("ffn1_norm_0", 8), ("ffn1_norm_1", 8), ("mix_norm_0", 8), ("mix_norm_1", 8),
                  ("ffn2_norm_0", 8), ("ffn2_norm_1", 8), ("final_norm", 8), ("norm_mix_w_2", 8),
                  ("norm_ffn_w_2", 8), ("norm_final_w_2", 8), ("ret_gn_w_2", 8), ("mla_q_norm_w_2", 3),
                  ("mla_kv_norm_w_2", 2), ("a_out_norm", 1), ("b_b_in", 12), ("b_b_out", 8)]:
    VEC_ROWS[_name] = VEC_N
    VEC_N += _n
CONV_N = 4 * A_QKV // P
NORM_OF = {"F0": "ffn1_norm_0", "A": "mix_norm_0", "F1": "ffn2_norm_0", "F2": "ffn1_norm_1", "B": "mix_norm_1",
           "F3": "ffn2_norm_1", "N": "final_norm", "R": "norm_mix_w_2", "F4": "norm_ffn_w_2", "end": "norm_final_w_2"}


def rope_tables(dim):
    half = dim // 2
    inv = np.float32(10000.0) ** (-np.arange(half, dtype=np.float32) / np.float32(half))
    ang = (np.arange(TOK, dtype=np.float32)[:, None] * inv[None, :]).astype(np.float64)
    return np.cos(ang).T.astype(np.float32), np.sin(ang).T.astype(np.float32)


def rotation(starts, half):
    m = np.zeros((P, P), np.float32)
    for s in starts:
        for i in range(half):
            m[s + half + i, s + i] = -1.0
            m[s + i, s + half + i] = 1.0
    return m


def constants():
    i = np.arange(P)
    part, free = i[:, None], i[None, :]
    t = {"ident": np.eye(P), "ones": np.ones((P, P)), "meanw": np.full((P, P), 1.0 / P)}
    t["cum"] = (part <= free) * 1.0
    t["a_mask"] = np.where(free >= part, 0.0, NEG)
    t["a_pair1"] = ((free % 2 == 1) & (part == free - 1)) * 1.0
    for s in (2, 4, 8, 16, 32, 64):
        t[f"a_lvl{s}"] = (((part // s) % 2 == 1) & (free // s == part // s - 1)) * 1.0
    causal = np.where(free <= part, 0.0, NEG)
    t["b_mask"] = np.concatenate([causal, np.where(free > part, 0.0, NEG), causal], 1)
    c, s = rope_tables(RDK)
    t["r_cos"], t["r_sin"] = np.concatenate([c] * 4, 0), np.concatenate([s] * 4, 0)
    c, s = rope_tables(ROPE)
    t["m_cos"], t["m_sin"] = np.concatenate([c] * 8, 0), np.concatenate([s] * 8, 0)
    t["r_rot"] = rotation((0, RDK), RDK // 2)
    t["m_rot"] = rotation((0, NOPE), ROPE // 2)
    j = np.arange(3 * P).reshape(3, P).T[:, :, None]
    t["r_dist"] = (np.arange(TOK)[None, None, :] - j).reshape(P, -1)
    return {k: np.ascontiguousarray(v, np.float32) for k, v in t.items()}


KEPT = ["ident", "ones", "meanw"]
TABLES_OF = {
    "A": ["cum", "a_mask", "a_pair1"] + [f"a_lvl{s}" for s in (2, 4, 8, 16, 32, 64)],
    "B": ["b_mask"],
    "R": ["r_cos", "r_sin", "m_cos", "m_sin", "r_rot", "m_rot", "r_dist"],
}


def build(nc, dram, out, stages=STAGES):
    ctx = ExitStack()
    with ctx:
        sem_of = {}

        def sem(name):
            if name not in sem_of:
                sem_of[name] = ctx.enter_context(nc.semaphore(name))
            return sem_of[name]

        arena_bytes = 212800 // 32 * 32
        ARENA0 = (nc.sbuf_base + 31) // 32 * 32
        ctx.enter_context(nc.sbuf_tensor("arena", [P, arena_bytes // 4], F32))
        cursor = [0]
        top = [0]

        def place(name, shape, dt=F32, at=None):
            size = 4 * int(np.prod(shape[1:]))
            off = cursor[0] if at is None else at
            if at is None:
                cursor[0] = off + (size + 31) // 32 * 32
            assert off + size <= arena_bytes, (name, off, size)
            top[0] = max(top[0], off + size)
            return nc.alloc_sbuf_tensor_at(name, list(shape), dt, offset=ARENA0 + off)

        BT = 4 * TOK
        raw = place("raw", [P, SLOTS, KB * WIDE])
        whi = place("whi", [P, SLOTS, KB * WIDE], R32)
        wlo = place("wlo", [P, SLOTS, KB * WIDE], R32)
        x = place("x", [P, KB, TOK])
        u_at = cursor[0]
        uhi = place("uhi", [P, KB, TOK], R32)
        ulo = place("ulo", [P, KB, TOK], R32)
        h_at = cursor[0]
        hhi = place("hhi", [P, HB, TOK], R32)
        hlo = place("hlo", [P, HB, TOK], R32)
        std = place("std", [P, TOK])
        rstd = place("rstd", [P, TOK])
        scr_at = cursor[0]
        sq = place("sq", [P, KB, TOK])
        gate_s = place("gate_s", [P, 2, TOK])
        up_s = place("up_s", [P, 2, TOK])
        gate_a = place("gate_a", [P, 2, TOK])
        hid = place("hid", [P, 2, TOK])
        vec = place("vec", [P, VEC_N])
        conv = place("conv", [P, CONV_N])
        eps_t = place("eps_t", [P, 8])
        kept = {n: place(n, [P, P]) for n in KEPT}
        ident, ones, meanw = kept["ident"], kept["ones"], kept["meanw"]
        m_at = cursor[0]
        ps = ctx.enter_context(nc.psum_tensor("ps", [P, 8, 512], F32))

        l_x = sem("l_x")
        slots, first_slot = [], {}
        for st in stages:
            first_slot[st] = len(slots)
            slots += STAGE_SLOTS[st]()

        w_landed = [sem(f"w_landed{i}") for i in range(SLOTS)]
        w_hi = sem("w_hi")
        w_lo = sem("w_lo")
        w_used = sem("w_used")

        def elems(g):
            return slots[g][2] * slots[g][4]

        def load_slot(sp, g, i=None, per=0, dcol=0):
            name, k0, nk, c0, wide = slots[g]
            s = g % SLOTS
            if g >= SLOTS or per:
                sp.wait_ge(w_lo, g - SLOTS + 1 + (per * i if per else 0))
            col = c0 + dcol * i if dcol else c0
            src = dram[name].rearrange("(k p) n -> p k n", p=P)[:, k0:k0 + nk, bass.ds(col, wide)]
            dst = raw[:, s, 0:nk * wide].rearrange("p (k n) -> p k n", k=nk)
            sp.dma_start(dst, src).then_inc(w_landed[s], 16)
            if g == 0 and not per:
                sp.wait_ge(l_x, 64)

        def round_slot(act, g, i=None, per=0, n=None):
            s, n = g % SLOTS, n or elems(g)
            step = per * i if per else 0
            act.wait_ge(w_landed[s], 16 * (g // SLOTS + 1) + (16 * (per // SLOTS) * i if per else 0))
            if g >= SLOTS:
                act.wait_ge(w_used, g - SLOTS + 1 + step)
            nc.scalar.activation(whi[:, s, 0:n], raw[:, s, 0:n], ACT.Copy).then_inc(w_hi, 1)

        def rest_slot(dve, g, i=None, per=0, n=None):
            s, n = g % SLOTS, n or elems(g)
            dve.wait_ge(w_hi, g + 1 + (per * i if per else 0))
            nc.vector.tensor_tensor(wlo[:, s, 0:n], raw[:, s, 0:n], whi[:, s, 0:n].bitcast(F32),
                                    ALU.subtract).then_inc(w_lo, 1)

        class Ahead:

            def __init__(self, eng, split):
                self.eng, self.split, self.done = eng, split, 0

            def to(self, g):
                while self.done < min(g, len(slots)):
                    self.split(self.eng, self.done)
                    self.done += 1

        def slot_blocks(pe, g, outs, rhs, widths=None, i=None, per=0, k_first=0, first=True, last=True, tok=None,
                        ready=None):
            name, k0, nk, c0, wide = slots[g]
            s = g % SLOTS
            pe.wait_ge(w_lo, g + 1 + (per * i if per else 0))
            c = 0
            for b, o in enumerate(outs):
                m = widths[b] if widths else P
                for k in range(nk):
                    if ready and b == 0 and k % ready[2] == 0:
                        pe.wait_ge(ready[0], ready[1] + k // ready[2] + 1)
                    w = slice(k * wide + c, k * wide + c + m)
                    hi, lo = rhs[0][:, k_first + k, tok], rhs[1][:, k_first + k, tok]
                    nc.tensor.matmul(o, whi[:, s, w], hi, start=(first and k == 0), stop=False)
                    nc.tensor.matmul(o, whi[:, s, w], lo, start=False, stop=False)
                    ins = nc.tensor.matmul(o, wlo[:, s, w], hi, start=False, stop=(last and k == nk - 1))
                c += m
            ins.then_inc(w_used, 1)

        norm_no = {}
        for st in list(stages) + ["end"]:
            norm_no[st] = len(norm_no)
        tok_of = {st: slice(0, TOK) if st in ("R", "F4") else slice(META, TOK) for st in STAGES}
        tok_of["end"] = slice(META, TOK)
        s_x = sem("s_x")
        s_uhi = sem("s_uhi")
        s_ulo = sem("s_ulo")
        s_sq = sem("s_sq")
        s_fold = sem("s_fold")
        s_sum = sem("s_sum")
        s_std = sem("s_std")
        s_rstd = sem("s_rstd")
        SUM_BANK = 7
        no_split = ("N", "end")

        def split_no(st):
            return sum(1 for q in norm_no if norm_no[q] < norm_no[st] and q not in no_split)

        def squares(act, st, c):
            tok, w0, n = tok_of[st], VEC_ROWS[NORM_OF[st if st in NORM_OF else "end"]], 4 * norm_no[st] + c
            act.wait_ge(s_x, n + 1)
            if st not in no_split:
                for b in range(2):
                    k = 2 * c + b
                    ins = nc.scalar.activation(uhi[:, k, tok], x[:, k, tok], ACT.Copy, scale=vec[:, w0 + k:w0 + k + 1])
                ins.then_inc(s_uhi, 1)
            if n >= 4:
                act.wait_ge(s_sum, 2 * norm_no[st])
            nc.scalar.activation(sq[:, 2 * c:2 * c + 2, tok], x[:, 2 * c:2 * c + 2, tok], ACT.Square).then_inc(s_sq, 1)

        def low_part(dve, st, c):
            tok, w0 = tok_of[st], VEC_ROWS[NORM_OF[st]]
            dve.wait_ge(s_uhi, 4 * split_no(st) + c + 1)
            for b in range(2):
                k = 2 * c + b
                ins = nc.vector.scalar_tensor_tensor(ulo[:, k, tok], x[:, k, tok], vec[:, w0 + k:w0 + k + 1],
                                                     uhi[:, k, tok].bitcast(F32), ALU.mult, ALU.subtract)
            ins.then_inc(s_ulo, 1)

        def fold_squares(pool, st):
            tok, n = tok_of[st], norm_no[st]
            for i, c in enumerate((1, 2)):
                pool.wait_ge(s_sq, 4 * n + c + 1)
                if i:
                    pool.wait_ge(s_fold, 3 * n + i)
                nc.gpsimd.tensor_tensor(sq[:, 0:2, tok], sq[:, 0:2, tok], sq[:, 2 * c:2 * c + 2, tok],
                                        ALU.add).then_inc(s_fold, 1)
            pool.wait_ge(s_fold, 3 * n + 2)
            nc.gpsimd.tensor_tensor(sq[:, 0, tok], sq[:, 0, tok], sq[:, 1, tok], ALU.add).then_inc(s_fold, 1)

        def add_squares(pe, st, last):
            tok, n = tok_of[st], norm_no[st]
            if last:
                pe.wait_ge(s_sq, 4 * n + 4)
            else:
                pe.wait_ge(s_fold, 3 * n + 3)
            for k in (6, 7) if last else (0,):
                ins = nc.tensor.matmul(ps[:, SUM_BANK, tok], ones[:, :], sq[:, k, tok], start=not last, stop=(k == 7))
            ins.then_inc(s_sum, 1)

        def x_split(st):
            return s_ulo, 4 * split_no(st), 2

        def sums(pe, st):
            add_squares(pe, st, False)
            add_squares(pe, st, True)

        def root(act, st):
            tok = tok_of[st]
            act.wait_ge(s_sum, 2 * norm_no[st] + 2)
            if norm_no[st]:
                act.wait_ge(s_rstd, norm_no[st])
            nc.scalar.activation(std[:, tok], ps[:, SUM_BANK, tok], ACT.Sqrt, scale=1.0 / D,
                                 bias=eps_t[:, 0:1]).then_inc(s_std, 1)

        def reciprocal_root(dve, st):
            tok = tok_of[st]
            dve.wait_ge(s_std, norm_no[st] + 1)
            nc.vector.reciprocal(rstd[:, tok], std[:, tok]).then_inc(s_rstd, 1)

        def over_pair(ap, shape):
            return ap.unsqueeze(1).broadcast_to(shape)

        s_gate = sem("s_gate")
        s_act = sem("s_act")
        s_up = sem("s_up")
        s_hid = sem("s_hid")
        s_hhi = sem("s_hhi")
        s_h = sem("s_h")
        ffn_no = {}
        for st in stages:
            if st[0] == "F":
                ffn_no[st] = len(ffn_no)

        def glu_banks(u):
            return 4 * (u % 2)

        def glu_products(pe, st, u, i=None, between=None, ready=None):
            g, tok, b0 = first_slot[st] + 2 * u, tok_of[st], glu_banks(u)
            per = 4 if i is not None else 0
            if u >= 1 or i is not None:
                pe.wait_ge(s_up, UNITS * ffn_no[st] + u + (2 * i if i is not None else 0))
            rhs = (uhi, ulo)
            slot_blocks(pe, g, [ps[:, b0 + b, tok] for b in range(2)], rhs, i=i, per=per, tok=tok, ready=ready)
            if between:
                between()
            slot_blocks(pe, g + 1, [ps[:, b0 + 2 + b, tok] for b in range(2)], rhs, i=i, per=per, tok=tok)

        def glu_silu(act, st, u, i=None):
            n, k = UNITS * ffn_no[st] + u, (2 * i if i is not None else 0)
            tok = tok_of[st]
            act.wait_ge(s_gate, n + 1 + k)
            if n + (1 if i is not None else 0) > 0:
                act.wait_ge(s_hid, n + k)
            nc.scalar.activation(gate_a[:, :, tok], gate_s[:, :, tok], ACT.Silu).then_inc(s_act, 1)

        def glu_hidden(dve, st, u, i=None):
            g, tok, b0 = first_slot[st] + 2 * u, tok_of[st], glu_banks(u)
            n, k, k4 = UNITS * ffn_no[st] + u, (2 * i if i is not None else 0), (4 * i if i is not None else 0)
            T = tok.stop - tok.start
            r = over_pair(rstd[:, tok], [P, 2, T])
            dve.wait_ge(w_used, g + 1 + k4)
            nc.vector.tensor_tensor(gate_s[:, :, tok], ps[:, b0:b0 + 2, tok], r, ALU.mult).then_inc(s_gate, 1)
            dve.wait_ge(w_used, g + 2 + k4)
            nc.vector.tensor_tensor(up_s[:, :, tok], ps[:, b0 + 2:b0 + 4, tok], r, ALU.mult).then_inc(s_up, 1)
            dve.wait_ge(s_act, n + 1 + k)
            dve.wait_ge(s_up, n + 2 + k)
            nc.vector.tensor_tensor(hid[:, :, tok], gate_a[:, :, tok], up_s[:, :, tok], ALU.mult).then_inc(s_hid, 1)
            dve.wait_ge(s_hid, n + 1 + k)
            blocks = bass.ds(2 * u + 4 * i, 2) if i is not None else slice(2 * u, 2 * u + 2)
            nc.vector.tensor_copy(hhi[:, blocks, tok], hid[:, :, tok]).then_inc(s_hhi, 1)
            dve.wait_ge(s_hhi, n + 1 + k)
            nc.vector.tensor_tensor(hlo[:, blocks, tok], hid[:, :, tok], hhi[:, blocks, tok].bitcast(F32),
                                    ALU.subtract).then_inc(s_h, 1)


        def out_g0(st, n_pair):
            return first_slot[st] + len(STAGE_SLOTS[st]()) - 4 * n_pair

        def out_banks(c):
            return 4 - 2 * (c % 2)

        def out_update(dve, st, nxt, c, n_pair, scale):
            g, tok, b0 = out_g0(st, n_pair) + n_pair * c, tok_of[st], out_banks(c)
            dve.wait_ge(w_used, g + n_pair)
            if st == "B":
                for b in range(2):
                    k = 2 * c + b
                    w = VEC_ROWS["b_b_out"] + k
                    ins = nc.vector.scalar_tensor_tensor(x[:, k, tok], ps[:, b0 + b, tok], vec[:, w:w + 1],
                                                         x[:, k, tok], ALU.add, ALU.add)
                ins.then_inc(s_x, 1)
                return
            xs = x[:, 2 * c:2 * c + 2, tok]
            nc.vector.scalar_tensor_tensor(xs, ps[:, b0:b0 + 2, tok], scale, xs, ALU.mult, ALU.add).then_inc(s_x, 1)

        def next_of(st):
            n = list(stages) + ["end"]
            return n[n.index(st) + 1]

        def ffn_load(sp, st):
            g0 = first_slot[st]
            for g in range(g0, g0 + 2 if g0 >= SLOTS else g0 + 6):
                load_slot(sp, g)
            lo = 0 if g0 >= SLOTS else 1
            with sp.Fori(lo, UNITS // 2) as i:
                for j in range(4):
                    load_slot(sp, g0 + 2 + j, i, per=4, dcol=2 * WIDE)
            with sp.Fori(0, 2) as i:
                for j in range(8):
                    load_slot(sp, g0 + 2 * UNITS + j, i, per=8, dcol=2 * WIDE)

        def ffn_act(act, st, ahead):
            g0, nxt = first_slot[st], next_of(st)
            ahead.to(g0 + 4)
            root(act, st)
            glu_silu(act, st, 0)
            with act.Fori(0, UNITS // 2) as i:
                for j in range(2):
                    for m in range(2):
                        round_slot(act, g0 + 4 + 2 * j + m, i, per=4, n=KB * WIDE)
                    glu_silu(act, st, 1 + j, i)
            ahead.done = g0 + 2 * UNITS + 2
            out_act(act, st, nxt, len(FFN_SPLIT), ahead)

        def out_act(act, st, nxt, n_pair, ahead):
            for c in range(4):
                ahead.to(out_g0(st, n_pair) + n_pair * (c + 1) + 2)
                squares(act, nxt, c)

        def ffn_dve(dve, st, ahead):
            g0, nxt = first_slot[st], next_of(st)
            ahead.to(g0 + 4)
            reciprocal_root(dve, st)
            dve.wait_ge(s_rstd, norm_no[st] + 1)
            glu_hidden(dve, st, 0)
            with dve.Fori(0, UNITS // 2) as i:
                for j in range(2):
                    for m in range(2):
                        rest_slot(dve, g0 + 4 + 2 * j + m, i, per=4, n=KB * WIDE)
                    glu_hidden(dve, st, 1 + j, i)
            ahead.done = g0 + 2 * UNITS + 2
            out_dve(dve, st, nxt, len(FFN_SPLIT), 1.0 if st == "F4" else 0.5, ahead)

        def out_dve(dve, st, nxt, n_pair, scale, ahead):
            for c in range(4):
                ahead.to(out_g0(st, n_pair) + n_pair * (c + 1) + 2)
                out_update(dve, st, nxt, c, n_pair, scale)
                if nxt not in no_split:
                    low_part(dve, nxt, c)

        def ffn_pe(pe, st):
            g0, tok, nxt = first_slot[st], tok_of[st], next_of(st)
            glu_products(pe, st, 0, between=lambda: sums(pe, st), ready=x_split(st))
            pe.wait_ge(s_std, norm_no[st] + 1)
            with pe.Fori(0, UNITS // 2) as i:
                for j in range(2):
                    glu_products(pe, st, 1 + j, i)
            gd, n0 = g0 + 2 * UNITS, UNITS * ffn_no[st]

            pe.wait_ge(s_up, n0 + UNITS)
            with pe.Fori(0, 2) as i:
                for c in range(2):
                    pe.wait_ge(s_x, 4 * norm_no[nxt] + c - 1 + 2 * i)
                    k, b0 = 0, out_banks(c)
                    for m, n in enumerate(FFN_SPLIT):
                        pe.wait_ge(s_h, n0 + (k + n + 1) // 2)
                        slot_blocks(pe, gd + 4 * c + m, [ps[:, b0 + b, tok] for b in range(2)], (hhi, hlo), tok=tok,
                                    i=i, per=8, k_first=k, first=(m == 0), last=(m == len(FFN_SPLIT) - 1))
                        k += n

        def out_pe(pe, st, splits, rhs, ready=None):
            g0, tok, nxt = out_g0(st, len(splits)), tok_of[st], next_of(st)
            for c in range(4):
                if c >= 2:
                    pe.wait_ge(s_x, 4 * norm_no[nxt] + c - 1)
                k, b0 = 0, out_banks(c)
                for m, n in enumerate(splits):
                    slot_blocks(pe, g0 + len(splits) * c + m, [ps[:, b0 + b, tok] for b in range(2)], rhs, tok=tok,
                                k_first=k, first=(m == 0), last=(m == len(splits) - 1), ready=ready if c == 0 else None)
                    k += n

        y = place("y", [P, KB, TOK], at=h_at)
        l_vec, l_ones, l_x, l_conv = sem("l_vec"), sem("l_ones"), sem("l_x"), sem("l_conv")
        s_y = sem("s_y")
        s_out = sem("s_out")

        def first_loads(act):
            act.dma_start(vec[:, :], dram["vectors"][:, 0:VEC_N]).then_inc(l_vec, 16)
            for c in range(4):
                act.dma_start(x[:, 2 * c:2 * c + 2, :], dram["x"][:, 2 * c:2 * c + 2, :]).then_inc(l_x, 16)
            act.dma_start(conv[:, :], dram["vectors"][:, VEC_N:]).then_inc(l_conv, 16)

        def other_loads(pool):
            for name in KEPT:
                pool.dma_start(kept[name][:, :], dram[name]).then_inc(l_ones, 16)

        def first_pe(pe):
            pe.wait_ge(l_ones, 48)

        def first_dve(dve, ahead):
            nc.vector.memset(eps_t[:, 0:1], EPS)
            nc.vector.memset(eps_t[:, 1:2], GN_EPS)
            nc.vector.memset(eps_t[:, 2:3], 1.0)
            nc.vector.memset(eps_t[:, 3:4], 0.0).then_inc(s_up, 1)
            ahead.to(1)
            dve.wait_ge(l_x, 64)
            nc.vector.memset(eps_t[:, 4:5], 0.0).then_inc(s_x, 4)
            for c in range(4):
                low_part(dve, stages[0], c)
            ahead.to(2)

        def first_act(act, ahead):
            act.wait_ge(l_vec, 16)
            act.wait_ge(s_up, 1)
            ahead.to(1)
            for c in range(4):
                squares(act, stages[0], c)
            ahead.to(2)
            act.wait_ge(l_conv, 16)

        def scaled_x(dve, st, dst, c):
            tok, w0 = tok_of[st], VEC_ROWS[NORM_OF[st]]
            for b in range(2):
                k = 2 * c + b
                ins = nc.vector.scalar_tensor_tensor(dst[:, k, tok], x[:, k, tok], vec[:, w0 + k:w0 + k + 1],
                                                     rstd[:, tok], ALU.mult, ALU.mult)
            return ins

        def norm_dve(dve):
            reciprocal_root(dve, "N")
            dve.wait_ge(s_rstd, norm_no["N"] + 1)
            nxt = next_of("N")
            for c in range(4):
                scaled_x(dve, "N", x, c).then_inc(s_x, 1)
            for c in range(4):
                if nxt not in no_split:
                    low_part(dve, nxt, c)

        def norm_pe(pe):
            sums(pe, "N")
            pe.wait_ge(s_std, norm_no["N"] + 1)

        def norm_act(act):
            root(act, "N")
            for c in range(4):
                squares(act, next_of("N"), c)

        def last_dve(dve):
            reciprocal_root(dve, "end")
            dve.wait_ge(s_rstd, norm_no["end"] + 1)
            for c in range(4):
                scaled_x(dve, "end", y, c).then_inc(s_y, 1)

        def last_pe(pe):
            sums(pe, "end")

        def last_act(act):
            root(act, "end")

        def last_store(sp):
            for c in range(4):
                sp.wait_ge(s_y, c + 1)
                sp.dma_start(out[:, 2 * c:2 * c + 2, :], y[:, 2 * c:2 * c + 2, META:]).then_inc(s_out, 16)
            sp.wait_ge(s_out, 64)

        mixer_load, mixer_pool, mixer_act, mixer_dve, mixer_pe = {}, {}, {}, {}, {}

        AG = 4
        a_off = [m_at]

        def small(name, shape, dt=F32):
            size = (4 * int(np.prod(shape[1:])) + 31) // 32 * 32
            t = place(name, shape, dt, at=a_off[0])
            a_off[0] += size
            return t

        if "A" in stages:
            a_tab = {n: small(f"at_{n}", [P, P]) for n in TABLES_OF["A"]}
            a_sz = small("a_sz", [P, AH, SEQ])
            a_dec = small("a_dec", [P, 2, 4, P])
            a_pre = place("a_pre", [P, 2, 2, SEQ + 4], at=scr_at + KB * BT)
            a_acc = place("a_acc", [P, 2, 2, SEQ], at=scr_at + KB * BT + 4 * 4 * (SEQ + 4))
            a_qkv = place("a_qkv", [P, 3 * AH, SEQ], at=h_at)
            a_vb = place("a_vb", [P, 2 * AH, P], at=h_at + 24576)
            a_LT = place("a_LT", [P, 2 * AH, P], at=h_at + 32768)
            a_dg = place("a_dg", [P, 2, 4, P], at=h_at + 40960)
            a_ba = place("a_ba", [P, SEQ], at=h_at + 45056)
            a_smalls = h_at + 46080
            a_kn = place("a_kn", [P, 2 * AH, P], at=h_at + 16384)
            a_sqk = place("a_sqk", [P, 2 * AH, SEQ], at=h_at + 24576)
            a_X = place("a_X", [P, 2 * AH, P], at=u_at)
            a_Y = place("a_Y", [P, 2 * AH, P], at=u_at + 8192)
            a_P = place("a_P", [P, 2 * AH, P], at=scr_at)
            a_AT = place("a_AT", [P, 2 * AH, P], at=scr_at + KB * BT)
            a_vn = place("a_vn", [P, 2 * AH, P], at=scr_at)
            a_S = place("a_S", [P, AH, P], at=u_at)
            a_wT = place("a_wT", [P, AH, P], at=u_at + 4096)
            a_O = place("a_O", [P, AH, SEQ], at=h_at + 32768)
            a_sqo = place("a_sqo", [P, AH, SEQ], at=scr_at + KB * BT)

            def tiny(name, shape):
                t = place(name, shape, at=tiny_at[0])
                tiny_at[0] += (4 * int(np.prod(shape[1:])) + 31) // 32 * 32
                return t

            tiny_at = [a_smalls]
            a_nat = tiny("a_nat", [P, 2, 16])
            a_beta = tiny("a_beta", [P, 2, AH])
            a_ad = tiny("a_ad", [P, 2, AH])
            a_e = tiny("a_e", [P, 2, AH])
            a_ln = tiny("a_ln", [P, 2, AH])
            a_g = tiny("a_g", [P, 2, AH])
            a_sp = tiny("a_sp", [P, 2, AH])
            a_G = tiny("a_G", [P, 4, AH])
            a_nG = tiny("a_nG", [P, 2, AH])
            a_eG = tiny("a_eG", [P, 2, AH])
            a_dl = tiny("a_dl", [P, AH])
            a_kd = tiny("a_kd", [P, AH])
            a_be = tiny("a_be", [P, AH])
            a_kc = tiny("a_kc", [P, 2, AH])
            a_sn = tiny("a_sn", [P, 4, AH])
            a_rn = tiny("a_rn", [P, 4, AH])
            a_rq = tiny("a_rq", [P, 2, AH])
            a_so = tiny("a_so", [P, 2, AH])
            a_ro = tiny("a_ro", [P, 2, AH])
            a_par = tiny("a_par", [P, 2, AH])
            a_eA = tiny("a_eA", [P, AH])
            assert tiny_at[0] <= h_at + 2 * HB * BT
            L_LEVELS = [2, 4, 8, 16, 32, 64]

        la_tab, la_par = sem("la_tab"), sem("la_par")
        sa = {n: sem("sa_" + n) if "A" in stages else None for n in (
            "in", "tap", "conv", "qkv", "z", "bat", "nat", "beta", "ad", "ab", "e", "ln", "eA", "sp", "g", "cum", "G",
            "eG", "dl", "kd", "kc", "sqk", "ss", "sn", "rn", "vt", "ve", "kt", "ke", "dg", "bc", "bcu", "dec", "kq", "kqu",
            "t1", "t1t", "p", "pm", "xy", "xyu", "x1", "scan", "scv", "sca", "sqo", "sso", "so", "ro", "o", "oh", "ol")}

        def quad(t, h0):
            return t[:, h0:h0 + 4, :]

        def bc4(ap):
            return ap.unsqueeze(1).broadcast_to([P, 4, P])

        def col4(ap):
            return ap.unsqueeze(2).broadcast_to([P, 4, P])

        BCASTS = [(g, kind) for g in range(AG) for kind in (["G", "beta", "rk", "rq"] + (["eG"] if g >= 2 else []))]
        BC_NO = {b: n for n, b in enumerate(BCASTS)}
        N_BC = len(BCASTS)
        OUT_ORDER = [(0, 0), (1, 0), (0, 1), (1, 1)]
        SCAN = [(step, q) for step in ("U0", "W", "S", "O0", "U1", "O1") for q in range(2)]
        ON_ACT = ("U0", "W", "U1")

        def scan_wait(eng, step, q):
            mine = [e for e in SCAN if (e[0] in ON_ACT) == (step in ON_ACT)]
            eng.wait_ge(sa["sca"] if step in ON_ACT else sa["scv"], mine.index((step, q)) + 1)

        def a_load(sp):
            for g in range(first_slot["A"], first_slot["A"] + len(STAGE_SLOTS["A"]())):
                load_slot(sp, g)

        def a_pool(pool):
            for n in TABLES_OF["A"]:
                pool.dma_start(a_tab[n][:, :], dram[n]).then_inc(la_tab, 16)
            pool.wait_ge(s_x, 4 * norm_no["A"] + 4)
            pool.dma_start(a_par[:, 0, :], dram["a_A_log"].broadcast_to([P, AH])).then_inc(la_par, 16)
            pool.dma_start(a_par[:, 1, :], dram["a_dt_bias"].broadcast_to([P, AH])).then_inc(la_par, 16)
            src = {"G": lambda g: a_G[:, g // 2, (g % 2) * 4:(g % 2) * 4 + 4],
                   "beta": lambda g: a_beta[:, g // 2, (g % 2) * 4:(g % 2) * 4 + 4],
                   "rk": lambda g: a_rn[:, 2 + g // 2, (g % 2) * 4:(g % 2) * 4 + 4],
                   "rq": lambda g: a_rq[:, g // 2, (g % 2) * 4:(g % 2) * 4 + 4],
                   "eG": lambda g: a_eG[:, g // 2, (g % 2) * 4:(g % 2) * 4 + 4]}
            pool.wait_ge(sa["G"], 1)
            pool.wait_ge(sa["eG"], 1)
            pool.wait_ge(sa["rn"], 2)
            pool.wait_ge(sa["beta"], 1)
            for n, (g, kind) in enumerate(BCASTS):
                if n >= 2:
                    pool.wait_ge(sa["bc"], n - 1)
                nc.gpsimd.tensor_tensor(a_dg[:, n % 2], bc4(ident[:, :]), col4(src[kind](g)), ALU.mult).then_inc(sa["dg"], 1)
            pool.wait_ge(sa["ro"], 1)
            for n, (t, q) in enumerate(OUT_ORDER, N_BC):
                pool.wait_ge(sa["bc"], n - 1)
                nc.gpsimd.tensor_tensor(a_dg[:, n % 2], bc4(ident[:, :]), col4(a_ro[:, t, 4 * q:4 * q + 4]),
                                        ALU.mult).then_inc(sa["dg"], 1)

        def a_pe(pe):
            g0, tok = first_slot["A"], tok_of["A"]
            for m in range(17):
                if m >= 3:
                    pe.wait_ge(sa["in"], m - 2)
                b0 = 2 * (m % 3)
                outs = [ps[:, b0 + b, 0:SEQ] for b in range(1 if m == 0 else 2)]
                slot_blocks(pe, g0 + m, outs, (uhi, ulo), tok=tok, ready=x_split("A") if m == 0 else None)
                if m == 0:
                    sums(pe, "A")
                if m == 2:
                    pe.wait_ge(sa["in"], 1)
                    for t in range(2):
                        ins = nc.tensor.transpose(ps[:, 6, t * P:t * P + P], a_ba[:, t * P:t * P + P], ident[:, :])
                    ins.then_inc(sa["bat"], 1)
                if m == 9:
                    pe.wait_ge(la_tab, 16 * len(TABLES_OF["A"]))
                    pe.wait_ge(sa["g"], 1)
                    for t in range(2):
                        nc.tensor.matmul(ps[:, 6, 8 * t:8 * t + 8], a_tab["cum"][:, :], a_g[:, t], start=True, stop=True)
                        ins = nc.tensor.matmul(ps[:, 6, 16 + 8 * t:24 + 8 * t], ones[:, :], a_g[:, t], start=True, stop=True)
                    ins.then_inc(sa["cum"], 1)
                if m == 13:
                    pe.wait_ge(sa["G"], 1)
                    pe.wait_ge(sa["sqk"], 8)
                    for w in range(2):
                        for t in range(2):
                            for h in range(AH):
                                c = (w * 2 + t) * AH + h
                                ins = nc.tensor.matmul(ps[:, 6, c:c + 1], a_sqk[:, w * AH + h, t * P:t * P + P],
                                                       ones[:, 0:1], start=True, stop=True)
                    ins.then_inc(sa["ss"], 1)
            pe.wait_ge(sa["in"], 17)
            for g in range(AG):
                for h in range(4):
                    hh = 2 * AH + (g % 2) * 4 + h
                    ins = nc.tensor.transpose(ps[:, g, h * P:h * P + P], a_qkv[:, hh, (g // 2) * P:(g // 2) * P + P], ident[:, :])
                ins.then_inc(sa["vt"], 1)
            for g in range(AG):
                bank = (4, 5, 0, 1)[g]
                if g >= 2:
                    pe.wait_ge(sa["ve"], g - 1)
                for h in range(4):
                    hh = AH + (g % 2) * 4 + h
                    ins = nc.tensor.transpose(ps[:, bank, h * P:h * P + P], a_qkv[:, hh, (g // 2) * P:(g // 2) * P + P],
                                              ident[:, :])
                ins.then_inc(sa["kt"], 1)
            pe.wait_ge(sa["ke"], 4)
            pe.wait_ge(sa["sn"], 1)

            def bcast(n):
                if n >= 2:
                    pe.wait_ge(sa["bcu"], n - 1)
                pe.wait_ge(sa["dg"], n + 1)
                nc.tensor.matmul(ps[:, 6 + n % 2, :], ones[:, :], a_dg[:, n % 2].rearrange("p a b -> p (a b)"),
                                 start=True, stop=True).then_inc(sa["bc"], 1)

            for g in range(AG):
                t, h0 = g // 2, (g % 2) * 4
                cols = slice(t * P, t * P + P)
                for kind in ("G", "beta", "rk", "rq"):
                    bcast(BC_NO[g, kind])
                pe.wait_ge(sa["bcu"], BC_NO[g, "rq"] + 1)
                if g >= 2:
                    pe.wait_ge(sa["kqu"], 2 * g - 2)
                for w in range(2):
                    for h in range(4):
                        ins = nc.tensor.matmul(ps[:, 2 * (g % 2) + w, h * P:h * P + P], a_qkv[:, AH + h0 + h, cols],
                                               a_qkv[:, (AH if w == 0 else 0) + h0 + h, cols], start=True, stop=True)
                    ins.then_inc(sa["kq"], 1)
                if t == 1:
                    bcast(BC_NO[g, "eG"])
            for g in range(AG):
                pe.wait_ge(sa["t1"], g + 1)
                for h in range(4):
                    ins = nc.tensor.transpose(ps[:, 2 + g, h * P:h * P + P], a_P[:, 4 * g + h], ident[:, :])
                ins.then_inc(sa["t1t"], 1)
            steps = len(L_LEVELS) * AG
            for q in range(steps + 2):
                if q < steps:
                    g, lvl = q % AG, q // AG
                    if lvl == 0:
                        pe.wait_ge(sa["x1"], g + 1)
                    else:
                        pe.wait_ge(sa["xyu"], q - AG + 1)
                    if q >= 3:
                        pe.wait_ge(sa["pm"], q - 2)
                    for h in range(4):
                        ins = nc.tensor.matmul(ps[:, (0, 1, 6)[q % 3], h * P:h * P + P], a_LT[:, 4 * g + h], a_X[:, 4 * g + h],
                                               start=True, stop=True)
                    ins.then_inc(sa["p"], 1)
                r = q - 2
                if r >= 0:
                    g, b0 = r % AG, 2 + 2 * (r % 2)
                    pe.wait_ge(sa["pm"], r + 1)
                    if r == 0:
                        pe.wait_ge(sa["x1"], 4)
                    if r >= 2:
                        pe.wait_ge(sa["xyu"], r - 1)
                    for h in range(4):
                        n = 4 * g + h
                        if r < steps - AG:
                            nc.tensor.matmul(ps[:, b0, h * P:h * P + P], a_Y[:, n], a_P[:, n], start=True, stop=True)
                        ins = nc.tensor.matmul(ps[:, b0 + 1, h * P:h * P + P], a_P[:, n], a_Y[:, n], start=True, stop=True)
                    ins.then_inc(sa["xy"], 1)
            pe.wait_ge(sa["xyu"], steps)
            for e, (step, q) in enumerate(SCAN):
                if e >= 8:
                    scan_wait(pe, *SCAN[e - 8])
                need = {"U0": (), "W": (), "S": ("U0",), "O0": ("U0",), "U1": ("W", "S"), "O1": ("U1", "S")}[step]
                for other in need:
                    scan_wait(pe, other, q)
                for h in range(4 * q, 4 * q + 4):
                    o = ps[:, e % 8, (h % 4) * P:(h % 4) * P + P]
                    pairs = {"U0": [(a_Y[:, h], a_vb[:, h])],
                             "W": [(a_kn[:, AH + h], a_Y[:, AH + h])],
                             "S": [(a_kn[:, h], a_vn[:, h])],
                             "O0": [(a_vn[:, h], a_AT[:, h])],
                             "U1": [(a_Y[:, AH + h], a_vb[:, AH + h]), (a_wT[:, h], a_S[:, h])],
                             "O1": [(a_S[:, h], a_qkv[:, h, P:SEQ]), (a_vn[:, AH + h], a_AT[:, AH + h])]}[step]
                    for i, (lhs, rhs) in enumerate(pairs):
                        ins = nc.tensor.matmul(o, lhs, rhs, start=(i == 0), stop=(i == len(pairs) - 1))
                ins.then_inc(sa["scan"], 1)
            scan_wait(pe, "O0", 1)
            pe.wait_ge(sa["sqo"], 1)
            for t in range(2):
                for h in range(AH):
                    ins = nc.tensor.matmul(ps[:, 0, t * AH + h:t * AH + h + 1], a_sqo[:, h, t * P:t * P + P], ones[:, 0:1],
                                           start=True, stop=True)
            ins.then_inc(sa["sso"], 1)
            for n in range(N_BC, N_BC + 4):
                bcast(n)
            out_pe(pe, "A", [8], (hhi, hlo), ready=(sa["ol"], 0, 4))

        def a_act(act, ahead):
            g0 = first_slot["A"]
            ahead.to(g0 + 3)
            root(act, "A")

            def finish(m):
                act.wait_ge(sa["conv"], 3 * m)
                nc.scalar.activation(a_qkv[:, 2 * m - 2:2 * m, :], a_acc[:, m % 2], ACT.Silu).then_inc(sa["qkv"], 1)

            for m in range(1, 17):
                if m == 6:
                    act.wait_ge(sa["nat"], 1)
                    nc.scalar.activation(a_beta[:, :, :], a_nat[:, :, 0:AH], ACT.Sigmoid).then_inc(sa["beta"], 1)
                    act.wait_ge(la_par, 32)
                    nc.scalar.activation(a_eA[:, :], a_par[:, 0, :], ACT.Exp).then_inc(sa["eA"], 1)
                    act.wait_ge(sa["ad"], 1)
                    nc.scalar.activation(a_e[:, :, :], a_ad[:, :, :], ACT.Abs).then_inc(sa["ab"], 1)
                    act.wait_ge(sa["ab"], 1)
                    nc.scalar.activation(a_e[:, :, :], a_e[:, :, :], ACT.Exp, scale=-1.0).then_inc(sa["e"], 1)
                    act.wait_ge(sa["e"], 1)
                    nc.scalar.activation(a_ln[:, :, :], a_e[:, :, :], ACT.Ln, bias=eps_t[:, 2:3]).then_inc(sa["ln"], 1)
                if m == 12:
                    act.wait_ge(sa["G"], 1)
                    nc.scalar.activation(a_eG[:, :, :], a_G[:, 0:2, :], ACT.Exp).then_inc(sa["eG"], 1)
                    act.wait_ge(sa["dl"], 1)
                    nc.scalar.activation(a_kd[:, :], a_dl[:, :], ACT.Exp).then_inc(sa["kd"], 1)
                ahead.to(g0 + m + 3)
                act.wait_ge(sa["in"], m + 1)
                if m <= 12:
                    for b in range(2):
                        ins = nc.scalar.activation(a_acc[:, m % 2, b], a_pre[:, m % 2, b, 0:SEQ], ACT.Copy,
                                                   scale=conv[:, 2 * m - 2 + b:2 * m - 1 + b])
                    ins.then_inc(sa["tap"], 1)
                else:
                    nc.scalar.activation(a_sz[:, 2 * (m - 13):2 * (m - 13) + 2, :], a_pre[:, m % 2, :, 3:SEQ + 3],
                                         ACT.Silu).then_inc(sa["z"], 1)
                if 2 <= m <= 13:
                    finish(m - 1)
                if 3 <= m <= 10:
                    b = 2 * (m - 3)
                    act.wait_ge(sa["qkv"], m - 2)
                    nc.scalar.activation(a_sqk[:, b:b + 2, :], a_qkv[:, b:b + 2, :], ACT.Square).then_inc(sa["sqk"], 1)
                if m == 15:
                    act.wait_ge(sa["ss"], 1)
                    nc.scalar.activation(a_sn[:, :, :], ps[:, 6, 0:32].rearrange("p (a b) -> p a b", b=AH), ACT.Sqrt,
                                         bias=eps_t[:, 0:1]).then_inc(sa["sn"], 1)
            for g in range(AG):
                act.wait_ge(sa["bcu"], BC_NO[g, "G"] + 1)
                for h in range(4):
                    c = (g % 2) * 4 + h
                    ins = nc.scalar.activation(a_dec[:, g % 2, h], a_dec[:, g % 2, h], ACT.Exp, bias=a_nG[:, g // 2, c:c + 1])
                ins.then_inc(sa["dec"], 1)
            for e, (step, q) in enumerate(SCAN):
                if step not in ON_ACT:
                    continue
                act.wait_ge(sa["scan"], e + 1)
                dst = {"U0": a_vn[:, 4 * q:4 * q + 4], "W": a_wT[:, 4 * q:4 * q + 4],
                       "U1": a_vn[:, AH + 4 * q:AH + 4 * q + 4]}[step]
                nc.scalar.activation(dst, ps[:, e % 8, :].rearrange("p (a b) -> p a b", b=P), ACT.Copy,
                                     scale=-1.0 if step == "W" else 1.0).then_inc(sa["sca"], 1)
            scan_wait(act, "O1", 1)
            nc.scalar.activation(a_sqo[:, :, :], a_O[:, :, :], ACT.Square).then_inc(sa["sqo"], 1)
            act.wait_ge(sa["sso"], 1)
            nc.scalar.activation(a_so[:, :, :], ps[:, 0, 0:16].rearrange("p (a b) -> p a b", b=AH), ACT.Sqrt, scale=1.0 / P,
                                 bias=eps_t[:, 0:1]).then_inc(sa["so"], 1)
            tok = tok_of["A"]
            for q in range(2):
                act.wait_ge(sa["o"], q + 1)
                nc.scalar.activation(hhi[:, 4 * q:4 * q + 4, tok], a_O[:, 4 * q:4 * q + 4, :], ACT.Copy).then_inc(sa["oh"], 1)
            out_act(act, "A", next_of("A"), 1, ahead)

        def a_dve(dve, ahead):
            g0, tok = first_slot["A"], tok_of["A"]
            ahead.to(g0 + 2)
            nc.vector.memset(a_pre[:, :, :, 0:3], 0.0)
            reciprocal_root(dve, "A")
            dve.wait_ge(s_rstd, norm_no["A"] + 1)
            r2 = over_pair(rstd[:, tok], [P, 2, SEQ])
            ahead.to(g0 + 3)

            def conv_of(m):
                for i in range(1, 4):
                    if i == 1:
                        dve.wait_ge(sa["tap"], m)
                    else:
                        dve.wait_ge(sa["conv"], 3 * (m - 1) + i - 1)
                    for b in range(2):
                        blk = 2 * m - 2 + b
                        ins = nc.vector.scalar_tensor_tensor(
                            a_acc[:, m % 2, b], a_pre[:, m % 2, b, i:i + SEQ],
                            conv[:, i * 24 + blk:i * 24 + blk + 1], a_acc[:, m % 2, b], ALU.mult, ALU.add)
                    ins.then_inc(sa["conv"], 1)

            for m in range(17):
                ahead.to(g0 + m + 3)
                b0 = 2 * (m % 3)
                dve.wait_ge(w_used, g0 + m + 1)
                if m == 0:
                    nc.vector.tensor_tensor(a_ba[:, :], ps[:, b0, 0:SEQ], rstd[:, tok], ALU.mult).then_inc(sa["in"], 1)
                else:
                    if m >= 15:
                        dve.wait_ge(sa["z"], m - 14)
                    nc.vector.tensor_tensor(a_pre[:, m % 2, :, 3:SEQ + 3], ps[:, b0:b0 + 2, 0:SEQ], r2,
                                            ALU.mult).then_inc(sa["in"], 1)
                if 2 <= m <= 13:
                    conv_of(m - 1)
                if m == 4:
                    dve.wait_ge(sa["bat"], 1)
                    nc.vector.tensor_copy(a_nat[:, :, :], ps[:, 6, 0:256].rearrange("p (t c) -> p t c", t=2)[:, :, P - 16:P]
                                          ).then_inc(sa["nat"], 1)
                    dve.wait_ge(sa["nat"], 1)
                    dve.wait_ge(la_par, 32)
                    nc.vector.tensor_tensor(a_ad[:, :, :], a_nat[:, :, AH:16], a_par[:, 1:2, :].broadcast_to([P, 2, AH]),
                                            ALU.add).then_inc(sa["ad"], 1)
                if m == 8:
                    dve.wait_ge(sa["ln"], 1)
                    nc.vector.scalar_tensor_tensor(a_sp[:, :, :], a_ad[:, :, :], 0.0, a_ln[:, :, :], ALU.max,
                                                   ALU.add).then_inc(sa["sp"], 1)
                    dve.wait_ge(sa["sp"], 1)
                    dve.wait_ge(sa["eA"], 1)
                    nc.vector.scalar_tensor_tensor(a_g[:, :, :], a_sp[:, :, :], -1.0,
                                                   a_eA[:, :].unsqueeze(1).broadcast_to([P, 2, AH]), ALU.mult,
                                                   ALU.mult).then_inc(sa["g"], 1)
                if m == 10:
                    dve.wait_ge(sa["cum"], 1)
                    nc.vector.tensor_copy(a_G[:, :, :], ps[:, 6, 0:32].rearrange("p (a b) -> p a b", b=AH)).then_inc(sa["G"], 1)
                    dve.wait_ge(sa["G"], 1)
                    nc.vector.tensor_scalar(a_nG[:, :, :], a_G[:, 0:2, :], -1.0, None, ALU.mult)
                    nc.vector.tensor_tensor(a_dl[:, :], a_G[:, 2, :], a_G[:, 0, :], ALU.subtract).then_inc(sa["dl"], 1)
                if m == 13:
                    dve.wait_ge(sa["eG"], 1)
                    dve.wait_ge(sa["beta"], 1)
                    nc.vector.tensor_tensor(a_be[:, :], a_beta[:, 1, :], a_eG[:, 1, :], ALU.mult).then_inc(sa["kc"], 1)
                if m == 16:
                    dve.wait_ge(sa["sn"], 1)
                    nc.vector.reciprocal(a_rn[:, :, :], a_sn[:, :, :]).then_inc(sa["rn"], 1)
                    dve.wait_ge(sa["rn"], 1)
                    nc.vector.tensor_scalar(a_rq[:, :, :], a_rn[:, 0:2, :], float(P) ** -0.5, None,
                                            ALU.mult).then_inc(sa["rn"], 1)
                    dve.wait_ge(sa["kd"], 1)
                    dve.wait_ge(sa["kc"], 1)
                    nc.vector.tensor_tensor(a_kc[:, 0, :], a_rn[:, 2, :], a_kd[:, :], ALU.mult)
                    nc.vector.tensor_tensor(a_kc[:, 1, :], a_rn[:, 3, :], a_be[:, :], ALU.mult).then_inc(sa["kc"], 1)
            for g in range(AG):
                t, h0 = g // 2, (g % 2) * 4
                dve.wait_ge(sa["vt"], g + 1)
                nc.vector.tensor_tensor(a_vb[:, 4 * g:4 * g + 4], ps[:, g, :].rearrange("p (a b) -> p a b", b=P),
                                        col4(a_beta[:, t, h0:h0 + 4]), ALU.mult).then_inc(sa["ve"], 1)
            dve.wait_ge(sa["kc"], 2)
            for g in range(AG):
                t, h0 = g // 2, (g % 2) * 4
                dve.wait_ge(sa["kt"], g + 1)
                nc.vector.tensor_tensor(a_kn[:, 4 * g:4 * g + 4], ps[:, (4, 5, 0, 1)[g], :].rearrange("p (a b) -> p a b", b=P),
                                        col4(a_kc[:, t, h0:h0 + 4]), ALU.mult).then_inc(sa["ke"], 1)
            dve.wait_ge(la_tab, 16 * len(TABLES_OF["A"]))

            def bank(n):
                return ps[:, 6 + n % 2, :].rearrange("p (a b) -> p a b", b=P)

            for g in range(AG):
                t, h0 = g // 2, (g % 2) * 4
                cols = slice(t * P, t * P + P)
                n = BC_NO[g, "G"]
                dve.wait_ge(sa["bc"], n + 1)
                if g >= 2:
                    dve.wait_ge(sa["kqu"], 2 * g - 2)
                nc.vector.tensor_tensor(a_dec[:, g % 2], bank(n), bc4(a_tab["a_mask"][:, :]), ALU.add).then_inc(sa["bcu"], 1)
                dve.wait_ge(sa["dec"], g + 1)
                dve.wait_ge(sa["bc"], n + 2)
                nc.vector.tensor_tensor(a_LT[:, 4 * g:4 * g + 4], bank(n + 1), a_dec[:, g % 2], ALU.mult).then_inc(sa["bcu"], 1)
                for i, w in enumerate((AH, 0)):
                    dve.wait_ge(sa["bc"], n + 3 + i)
                    kq = a_qkv[:, w + h0:w + h0 + 4, cols]
                    nc.vector.tensor_tensor(kq, bank(n + 2 + i), kq, ALU.mult).then_inc(sa["bcu"], 1)
                for w, dst in enumerate((a_LT, a_AT)):
                    dve.wait_ge(sa["kq"], 2 * g + w + 1)
                    if w == 0:
                        dve.wait_ge(sa["bcu"], n + 2)
                    other = a_LT[:, 4 * g:4 * g + 4] if w == 0 else a_dec[:, g % 2]
                    nc.vector.tensor_tensor(dst[:, 4 * g:4 * g + 4], ps[:, 2 * (g % 2) + w, :].rearrange("p (a b) -> p a b", b=P),
                                            other, ALU.mult).then_inc(sa["kqu"], 1)
                if t == 1:
                    dve.wait_ge(sa["bc"], n + 5)
                    qs = a_qkv[:, h0:h0 + 4, cols]
                    nc.vector.tensor_tensor(qs, bank(n + 4), qs, ALU.mult).then_inc(sa["bcu"], 1)
            for g in range(AG):
                s4 = slice(4 * g, 4 * g + 4)
                dve.wait_ge(sa["kqu"], 2 * g + 1)
                nc.vector.tensor_tensor(a_P[:, s4], a_LT[:, s4], bc4(a_tab["a_pair1"][:, :]), ALU.mult).then_inc(sa["t1"], 1)
                dve.wait_ge(sa["t1"], g + 1)
                nc.vector.tensor_tensor(a_Y[:, s4], bc4(ident[:, :]), a_P[:, s4], ALU.subtract)
            for g in range(AG):
                s4 = slice(4 * g, 4 * g + 4)
                dve.wait_ge(sa["t1t"], g + 1)
                nc.vector.tensor_tensor(a_X[:, s4], bc4(ident[:, :]), ps[:, 2 + g, :].rearrange("p (a b) -> p a b", b=P),
                                        ALU.subtract).then_inc(sa["x1"], 1)
            steps = len(L_LEVELS) * AG
            for q in range(steps + 2):
                if q < steps:
                    s4 = slice(4 * (q % AG), 4 * (q % AG) + 4)
                    dve.wait_ge(sa["p"], q + 1)
                    nc.vector.tensor_tensor(a_P[:, s4], ps[:, (0, 1, 6)[q % 3], :].rearrange("p (a b) -> p a b", b=P),
                                            bc4(a_tab[f"a_lvl{L_LEVELS[q // AG]}"][:, :]), ALU.mult).then_inc(sa["pm"], 1)
                r = q - 2
                if r >= 0:
                    s4, b0 = slice(4 * (r % AG), 4 * (r % AG) + 4), 2 + 2 * (r % 2)
                    dve.wait_ge(sa["xy"], r + 1)
                    if r < steps - AG:
                        nc.vector.tensor_tensor(a_X[:, s4], a_X[:, s4], ps[:, b0, :].rearrange("p (a b) -> p a b", b=P),
                                                ALU.subtract)
                    nc.vector.tensor_tensor(a_Y[:, s4], a_Y[:, s4], ps[:, b0 + 1, :].rearrange("p (a b) -> p a b", b=P),
                                            ALU.subtract).then_inc(sa["xyu"], 1)
            for e, (step, q) in enumerate(SCAN):
                if step in ON_ACT:
                    continue
                dve.wait_ge(sa["scan"], e + 1)
                dst = {"S": a_S[:, 4 * q:4 * q + 4], "O0": a_O[:, 4 * q:4 * q + 4, 0:P], "O1": a_O[:, 4 * q:4 * q + 4, P:SEQ]}[step]
                nc.vector.tensor_copy(dst, ps[:, e % 8, :].rearrange("p (a b) -> p a b", b=P)).then_inc(sa["scv"], 1)
            dve.wait_ge(sa["so"], 1)
            nc.vector.reciprocal(a_ro[:, :, :], a_so[:, :, :]).then_inc(sa["ro"], 1)
            w = VEC_ROWS["a_out_norm"]
            for n, (t, q) in enumerate(OUT_ORDER, N_BC):
                dve.wait_ge(sa["bc"], n + 1)
                o = a_O[:, 4 * q:4 * q + 4, t * P:t * P + P]
                nc.vector.tensor_tensor(o, bank(n), o, ALU.mult).then_inc(sa["bcu"], 1)
                if t == 1:
                    dve.wait_ge(sa["bcu"], n + 1)
                    dve.wait_ge(sa["z"], 4)
                    o = a_O[:, 4 * q:4 * q + 4, :]
                    nc.vector.scalar_tensor_tensor(o, o, vec[:, w:w + 1], a_sz[:, 4 * q:4 * q + 4, :], ALU.mult,
                                                   ALU.mult).then_inc(sa["o"], 1)
            for q in range(2):
                dve.wait_ge(sa["oh"], q + 1)
                nc.vector.tensor_tensor(hlo[:, 4 * q:4 * q + 4, tok], a_O[:, 4 * q:4 * q + 4, :],
                                        hhi[:, 4 * q:4 * q + 4, tok].bitcast(F32), ALU.subtract).then_inc(sa["ol"], 1)
            out_dve(dve, "A", next_of("A"), 1, 1.0, ahead)

        mixer_load["A"], mixer_pool["A"], mixer_act["A"], mixer_dve["A"], mixer_pe["A"] = a_load, a_pool, a_act, a_dve, a_pe

        BS = 3 * P
        if "B" in stages:
            b_mask = place("b_mask", [P, BS], at=m_at)
            b_ol = place("b_ol", [P, KB, TOK], R32, at=m_at + 4 * BS)
            b_oh = place("b_oh", [P, KB, TOK], R32, at=scr_at + KB * BT)
            b_q = place("b_q", [P, KB, SEQ], at=h_at)
            b_kt = place("b_kt", [P, 2, SEQ], at=h_at + 8192)
            b_vt = place("b_vt", [P, 2, SEQ], at=h_at + 10240)
            b_kd = place("b_kd", [P, BKV, SEQ], at=h_at + 12288)
            b_vn = place("b_vn", [P, 2, BKV * BD], at=h_at + 16384)
            b_s = place("b_s", [P, 2, BS], at=h_at + 18432)
            b_p = place("b_p", [P, 3, BS], at=h_at + 21504)
            b_pt = place("b_pt", [P, 2, BS], at=h_at + 26112)
            b_tmp = place("b_tmp", [P, 2, 2, SEQ], at=h_at + 33024)
            b_st = place("b_st", [P, 6, BH, 2], at=h_at + 31744)
            b_sink = place("b_sink", [P, BH], at=h_at + 32768)
            b_mx, b_nm, b_sum, b_es, b_den, b_r = [b_st[:, i] for i in range(6)]
        sbn = {n: sem("sb_" + n) if "B" in stages else None for n in ("tab", "snk", "in", "bias", "kd", "vt", "vn", "s", "sm", "mx", "nm", "ex", "den",
                                           "r", "p", "pt", "ptc", "o", "oh", "ol")}

        def b_load(sp):
            for g in range(first_slot["B"], first_slot["B"] + len(STAGE_SLOTS["B"]())):
                load_slot(sp, g)

        def b_pool(pool):
            pool.wait_ge(s_x, 4 * norm_no["B"] + 4)
            pool.dma_start(b_mask[:, :], dram["b_mask"]).then_inc(sbn["tab"], 16)
            pool.dma_start(b_sink[:, :], dram["b_sinks"].broadcast_to([P, BH])).then_inc(sbn["snk"], 16)
            pool.wait_ge(sbn["tab"], 16)
            pool.wait_ge(sbn["snk"], 16)

        def b_pe(pe):
            g0, tok = first_slot["B"], tok_of["B"]
            for m in range(6):
                if m >= 3:
                    pe.wait_ge(sbn["in"], m - 2)
                b0 = 2 * (m % 3)
                slot_blocks(pe, g0 + m, [ps[:, b0 + b, 0:SEQ] for b in range(2)], (uhi, ulo), tok=tok,
                            ready=x_split("B") if m == 0 else None)
                if m == 0:
                    sums(pe, "B")
                if m == 3:
                    pe.wait_ge(sbn["bias"], 4)
                    pe.wait_ge(s_std, norm_no["B"] + 1)
                    for t in range(2):
                        for b in range(2):
                            c = (2 * t + b) * P
                            ins = nc.tensor.transpose(ps[:, 7, c:c + P], b_vt[:, b, t * P:t * P + P], ident[:, :])
                    ins.then_inc(sbn["vt"], 1)
            pe.wait_ge(sbn["kd"], 1)
            pe.wait_ge(sbn["in"], 5)
            for h in range(BH + 3):
                if h == 2:
                    pe.wait_ge(sbn["in"], 6)
                if h < BH:
                    off, kv = BD * (h % 2), h // 4
                    if h % 2 == 0:
                        pe.wait_ge(sbn["bias"], 5 + h // 2)
                    if h >= 3:
                        pe.wait_ge(sbn["sm"], h - 2)
                    r = slice(off, off + BD)
                    nc.tensor.matmul(ps[:, h % 3, 0:P], b_q[r, h // 2, 0:P], b_kd[r, kv, 0:P], start=True, stop=True)
                    nc.tensor.matmul(ps[:, h % 3, P:BS], b_q[r, h // 2, P:SEQ], b_kd[r, kv, :], start=True,
                                     stop=True).then_inc(sbn["s"], 1)
                if 2 <= h <= BH + 1:
                    g = h - 2
                    pe.wait_ge(sbn["p"], g + 1)
                    if g >= 2:
                        pe.wait_ge(sbn["ptc"], g - 1)
                    for i in range(3):
                        ins = nc.tensor.transpose(ps[:, 3 + g % 2, i * P:i * P + P], b_p[:, g % 3, i * P:i * P + P], ident[:, :])
                    ins.then_inc(sbn["pt"], 1)
                if h >= 3:
                    g = h - 3
                    pair, r, kv = g // 2, slice(BD * (g % 2), BD * (g % 2) + BD), g // 4
                    pe.wait_ge(sbn["ptc"], g + 1)
                    if g == 0:
                        pe.wait_ge(sbn["vn"], 1)
                    if pair >= 2:
                        pe.wait_ge(sbn["ol"], pair - 1)
                    o = ps[r, 5 + pair % 2, :]
                    v = slice(kv * BD, kv * BD + BD)
                    nc.tensor.matmul(o[:, 0:P], b_vn[:, 0, v], b_pt[:, g % 2, 0:P], start=True, stop=True)
                    nc.tensor.matmul(o[:, P:SEQ], b_vn[:, 0, v], b_pt[:, g % 2, P:2 * P], start=True, stop=False)
                    nc.tensor.matmul(o[:, P:SEQ], b_vn[:, 1, v], b_pt[:, g % 2, 2 * P:BS], start=False,
                                     stop=True).then_inc(sbn["o"], 1)
            out_pe(pe, "B", [8], (b_oh, b_ol), ready=(sbn["ol"], 0, 1))

        def b_act(act, ahead):
            g0, tok = first_slot["B"], tok_of["B"]
            ahead.to(g0 + 3)
            root(act, "B")
            for m in range(6):
                ahead.to(g0 + m + 3)
                act.wait_ge(sbn["in"], m + 1)
                for b in range(2):
                    o = B_ORDER[m]
                    w = VEC_ROWS["b_b_in"] + 2 * o + b
                    dst = b_q[:, 2 * o + b] if o < 4 else (b_kt if o == 4 else b_vt)[:, b]
                    nc.scalar.activation(dst, b_tmp[:, m % 2, b], ACT.Identity, bias=vec[:, w:w + 1]).then_inc(sbn["bias"], 1)
            act.wait_ge(sbn["snk"], 16)
            for h in range(BH + 4):
                if h < BH:
                    act.wait_ge(sbn["nm"], h + 1)
                    if h >= 3:
                        act.wait_ge(sbn["pt"], h - 2)
                    nc.scalar.activation(b_es[:, h], b_nm[:, h], ACT.Exp, bias=b_sink[:, h:h + 1])
                    for t, c in enumerate((slice(0, P), slice(P, BS))):
                        ins = nc.scalar.activation(b_p[:, h % 3, c], b_s[:, h % 2, c], ACT.Exp, bias=b_nm[:, h, t:t + 1],
                                                   accum_out=b_sum[:, h, t:t + 1])
                    ins.then_inc(sbn["ex"], 1)
                if 2 <= h <= BH + 1:
                    g = h - 2
                    act.wait_ge(sbn["pt"], g + 1)
                    if g >= 2:
                        act.wait_ge(sbn["o"], g - 1)
                    nc.scalar.activation(b_pt[:, g % 2], ps[:, 3 + g % 2, 0:BS], ACT.Copy).then_inc(sbn["ptc"], 1)
                if h >= 5 and h % 2 == 1:
                    pair = (h - 5) // 2
                    act.wait_ge(sbn["o"], 2 * pair + 2)
                    nc.scalar.activation(b_oh[:, pair, tok], ps[:, 5 + pair % 2, 0:SEQ], ACT.Copy).then_inc(sbn["oh"], 1)
            out_act(act, "B", next_of("B"), 1, ahead)

        def b_dve(dve, ahead):
            g0, tok = first_slot["B"], tok_of["B"]
            ahead.to(g0 + 3)
            reciprocal_root(dve, "B")
            dve.wait_ge(s_rstd, norm_no["B"] + 1)
            r2 = over_pair(rstd[:, tok], [P, 2, SEQ])
            for m in range(6):
                ahead.to(g0 + m + 3)
                dve.wait_ge(w_used, g0 + m + 1)
                if m >= 2:
                    dve.wait_ge(sbn["bias"], 2 * m - 2)
                nc.vector.tensor_tensor(b_tmp[:, m % 2], ps[:, 2 * (m % 3):2 * (m % 3) + 2, 0:SEQ], r2,
                                        ALU.mult).then_inc(sbn["in"], 1)
                if m == 2:
                    dve.wait_ge(sbn["bias"], 2)
                    for kv in range(BKV):
                        src = b_kt[BD * (kv % 2):BD * (kv % 2) + BD, kv // 2]
                        nc.vector.tensor_copy(b_kd[0:BD, kv], src)
                        ins = nc.vector.tensor_copy(b_kd[BD:P, kv], src)
                    ins.then_inc(sbn["kd"], 1)
                if m == 4:
                    dve.wait_ge(sbn["vt"], 1)
                    nc.vector.tensor_copy(b_vn[:, :, :], ps[:, 7, :].rearrange("p (t c) -> p t c", t=2)).then_inc(sbn["vn"], 1)
            dve.wait_ge(sbn["tab"], 16)
            dve.wait_ge(sbn["snk"], 16)
            for h in range(BH + 4):
                if h < BH:
                    dve.wait_ge(sbn["s"], h + 1)
                    if h >= 2:
                        dve.wait_ge(sbn["ex"], h - 1)
                    nc.vector.scalar_tensor_tensor(b_s[:, h % 2], ps[:, h % 3, 0:BS], BD ** -0.5, b_mask[:, :], ALU.mult,
                                                   ALU.add).then_inc(sbn["sm"], 1)
                    dve.wait_ge(sbn["sm"], h + 1)
                    nc.vector.tensor_reduce(b_mx[:, h, 0:1], b_s[:, h % 2, 0:P], AX.X, ALU.max)
                    nc.vector.tensor_reduce(b_mx[:, h, 1:2], b_s[:, h % 2, P:BS], AX.X, ALU.max).then_inc(sbn["mx"], 1)
                    dve.wait_ge(sbn["mx"], h + 1)
                    nc.vector.tensor_scalar(b_nm[:, h], b_mx[:, h], b_sink[:, h:h + 1], -1.0, ALU.max,
                                            ALU.mult).then_inc(sbn["nm"], 1)
                if 1 <= h <= BH:
                    g = h - 1
                    dve.wait_ge(sbn["ex"], g + 1)
                    nc.vector.tensor_tensor(b_den[:, g], b_sum[:, g], b_es[:, g], ALU.add).then_inc(sbn["den"], 1)
                    dve.wait_ge(sbn["den"], g + 1)
                    nc.vector.reciprocal(b_r[:, g], b_den[:, g]).then_inc(sbn["r"], 1)
                    dve.wait_ge(sbn["r"], g + 1)
                    for t, c in enumerate((slice(0, P), slice(P, BS))):
                        ins = nc.vector.tensor_scalar(b_p[:, g % 3, c], b_p[:, g % 3, c], b_r[:, g, t:t + 1], None, ALU.mult)
                    ins.then_inc(sbn["p"], 1)
                if h >= 5 and h % 2 == 1:
                    pair = (h - 5) // 2
                    dve.wait_ge(sbn["oh"], pair + 1)
                    nc.vector.tensor_tensor(b_ol[:, pair, tok], ps[:, 5 + pair % 2, 0:SEQ], b_oh[:, pair, tok].bitcast(F32),
                                            ALU.subtract).then_inc(sbn["ol"], 1)
            out_dve(dve, "B", next_of("B"), 1, 1.0, ahead)

        mixer_load["B"], mixer_pool["B"], mixer_act["B"], mixer_dve["B"], mixer_pe["B"] = b_load, b_pool, b_act, b_dve, b_pe

        JT = [0, 1, 2]
        if "R" in stages:
            r_cur = [m_at]

            def r_at(n_bytes):
                at = r_cur[0]
                r_cur[0] += (n_bytes + 31) // 32 * 32
                return at

            r_tab = {n: place(f"rt_{n}", [P, 3, TOK] if n == "r_dist" else [P, P] if n.endswith("rot") else [P, TOK],
                              at=r_at(3 * BT if n == "r_dist" else 4 * P if n.endswith("rot") else BT))
                     for n in TABLES_OF["R"]}
            r_z = r_at(6 * BT)
            r_kr = place("r_kr", [P, TOK], at=r_at(BT))
            r_lg = place("r_lg", [P, 2, RH], at=r_at(64))
            r_par = place("r_par", [P, 2, RH], at=r_at(64))
            r_st = place("r_st", [P, 4, MH, 3], at=r_at(384))
            assert r_cur[0] <= arena_bytes
            r_c = place("r_c", [P, 5, TOK], at=r_z)
            r_vm = place("r_vm", [P, 3, MH * MDV], at=r_z)
            hb = lambda n: h_at + n * BT
            r_q = place("r_q", [P, 8, TOK], at=hb(0))
            r_v = place("r_v", [P, 3, RH * RDV], at=hb(8))
            r_srg = place("r_srg", [P, 8, TOK], at=hb(20))
            r_gr = place("r_gr", [P, 8, TOK], at=hb(28))
            r_gm = place("r_gm", [P, 8, TOK], at=hb(36))
            r_t = place("r_t", [P, 2, 2, TOK], at=scr_at + 12 * BT)
            r_t2 = place("r_t2", [P, 2, 2, TOK], at=scr_at + 8 * BT)
            r_W = place("r_W", [P, 2, 3, TOK], at=scr_at)
            r_s = place("r_s", [P, 3, TOK], at=scr_at + 6 * BT)
            r_e = place("r_e", [P, 3, TOK], at=scr_at + 9 * BT)
            r_y = r_q
            y_of = lambda h: h // 2 + 4 * (h % 2)
            r_yh = place("r_yh", [P, 8, TOK], R32, at=u_at + 8 * BT)
            r_yl = place("r_yl", [P, 8, TOK], R32, at=u_at)
            r_ysq = place("r_ysq", [P, 2, TOK], at=scr_at)
            r_sd = place("r_sd", [P, 2, TOK], at=scr_at + 2 * BT)
            r_cqh = place("r_cqh", [P, 3, TOK], R32, at=hb(8))
            r_cql = place("r_cql", [P, 3, TOK], R32, at=hb(11))
            r_ckh = place("r_ckh", [P, 2, 3 * P], R32, at=hb(14))
            r_ckl = place("r_ckl", [P, 2, 3 * P], R32, at=hb(17))
            r_qc = place("r_qc", [P, MH, TOK], at=hb(20))
            r_kc = place("r_kc", [P, MH, TOK], at=hb(0))
            r_csq = place("r_csq", [P, 5, TOK], at=scr_at)
            r_csd = place("r_csd", [P, 2, TOK], at=scr_at + 5 * BT)
            r_rt = place("r_rt", [P, 2, 4, TOK], at=scr_at + 8 * BT)
            r_p = place("r_p", [P, 2, 3, TOK], at=scr_at)
            r_pt = place("r_pt", [P, 2, 3, TOK], at=scr_at + 6 * BT)
            r_oh = place("r_oh", [P, 4, TOK], R32, at=hb(8))
            r_ol = place("r_ol", [P, 4, TOK], R32, at=hb(12))
            r_mh = place("r_mh", [P, 8, TOK], R32, at=hb(0))
            r_ml = place("r_ml", [P, 8, TOK], R32, at=hb(20))
        sr = {n: sem("sr_" + n) if "R" in stages else None for n in (
            "tab", "par", "in", "act", "rot", "rope", "vt", "vc", "zeros", "lg", "e", "w", "wx", "s", "sd", "o", "yc",
            "mu", "yd", "ysq", "var", "sdv", "rec", "yn", "yh", "yl", "gr", "rb", "csq", "csum", "csd", "cr", "cn", "ch", "cl",
            "qc", "qrot", "qr", "qrd", "kc", "vm", "sm", "mx", "nm", "ex", "rs", "p", "pt", "ptc", "pta", "ov", "oh", "ol", "gm", "mh", "ml")}
        IN_R = len(mixer_r_in_slots())

        def r_load(sp):
            for g in range(first_slot["R"], first_slot["R"] + len(STAGE_SLOTS["R"]())):
                load_slot(sp, g)

        def r_pool(pool):
            pool.wait_ge(s_x, 4 * norm_no[next_of("B") if "B" in stages else "R"] + 4)
            for n in TABLES_OF["R"]:
                dst = r_tab[n][:, :, :].rearrange("p a b -> p (a b)") if n == "r_dist" else r_tab[n][:, :]
                pool.dma_start(dst, dram[n]).then_inc(sr["tab"], 16)
            pool.dma_start(r_par[:, 0, :], dram["ret_decay_fwd_2"].broadcast_to([P, RH])).then_inc(sr["par"], 16)
            pool.dma_start(r_par[:, 1, :], dram["ret_decay_bwd_2"].broadcast_to([P, RH])).then_inc(sr["par"], 16)
            pool.wait_ge(sr["tab"], 16 * len(TABLES_OF["R"]))
            pool.wait_ge(sr["lg"], 1)
            pool.wait_ge(sr["rope"], 5)
            for h in range(RH):
                if h >= 1:
                    pool.wait_ge(sr["w"], h)
                nc.gpsimd.tensor_scalar(r_e[:, :, :], r_tab["r_dist"][:, :, :], r_lg[:, 1, h:h + 1], None,
                                        ALU.mult).then_inc(sr["e"], 1)
            pool.wait_ge(sr["o"], RH)
            nc.gpsimd.memset(r_ckh[:, :, TOK:].bitcast(F32), 0.0)
            nc.gpsimd.memset(r_ckl[:, :, TOK:].bitcast(F32), 0.0).then_inc(sr["zeros"], 1)

        def in_bank(m):
            return 4 + 2 * (m % 2) if m >= 16 else 2 * (m % 3)

        def r_pe(pe):
            g0, tok = first_slot["R"], tok_of["R"]

            def head_output(g):
                pe.wait_ge(sr["sd"], g + 1)
                if g >= 1:
                    pe.wait_ge(sr["yc"], g)
                for t, (j0, n) in enumerate(TILES):
                    ins = nc.tensor.matmul(ps[:, 3, tok], r_v[0:n, t, g * RDV:g * RDV + RDV], r_s[0:n, t, :],
                                           start=(t == 0), stop=(t == 2))
                ins.then_inc(sr["o"], 1)

            for m in range(IN_R):
                if m >= 18:
                    pe.wait_ge(sr["in"], m - 1)
                elif m >= 3:
                    pe.wait_ge(sr["in"], m - 2)
                if m == 16:
                    pe.wait_ge(sr["in"], 15)
                if m == 17:
                    pe.wait_ge(sr["csd"], 1)
                b0 = in_bank(m)
                slot_blocks(pe, g0 + m, [ps[:, b0 + b, tok] for b in range(slots[g0 + m][4] // P)], (uhi, ulo), tok=tok,
                            ready=x_split("R") if m == 0 else None)
                if m == 0:
                    sums(pe, "R")
                if m == 1:
                    pe.wait_ge(sr["tab"], 16 * len(TABLES_OF["R"]))
                    pe.wait_ge(s_std, norm_no["R"] + 1)
                if 1 <= m <= 4:
                    pe.wait_ge(sr["in"], m)
                    if m >= 2:
                        pe.wait_ge(sr["rope"], m - 1)
                    for b in range(2):
                        ins = nc.tensor.matmul(ps[:, 6 + b, tok], r_tab["r_rot"][:, :], r_t[:, (m - 1) % 2, b, :],
                                               start=True, stop=True)
                    ins.then_inc(sr["rot"], 1)
                if 5 <= m <= 8:
                    pe.wait_ge(sr["in"], m)
                    if m == 5:
                        pe.wait_ge(sr["rope"], 4)
                    else:
                        pe.wait_ge(sr["vc"], m - 5)
                    for b in range(2):
                        for t, (i0, n) in enumerate(TILES):
                            ins = nc.tensor.transpose(ps[0:n, 6 + b, t * P:t * P + P], r_t[:, (m - 1) % 2, b, i0:i0 + n],
                                                      ident[:, :])
                    ins.then_inc(sr["vt"], 1)
                if m == 12:
                    pe.wait_ge(sr["in"], 12)
                    pe.wait_ge(sr["vc"], 4)
                    nc.tensor.matmul(ps[0:ROPE, 6, tok], r_tab["m_rot"][0:ROPE, 0:ROPE], r_t[0:ROPE, 1, 0, :], start=True,
                                     stop=True).then_inc(sr["rot"], 1)
                if m == 13:
                    pe.wait_ge(sr["csq"], 1)
                    pe.wait_ge(sr["rope"], 5)
                    for b in range(5):
                        ins = nc.tensor.matmul(ps[:, 6 + b // 3, tok], ones[:, :], r_csq[:, b, :], start=(b in (0, 3)),
                                               stop=(b in (2, 4)))
                    ins.then_inc(sr["csum"], 1)
                if m >= 16:
                    h = m - 16
                    r = slice(RDK * (h % 2), RDK * (h % 2) + RDK)
                    if h == 0:
                        pe.wait_ge(sr["in"], 16)
                    else:
                        pe.wait_ge(sr["sd"], h)
                    for t, (j0, n) in enumerate(TILES):
                        ins = nc.tensor.matmul(ps[0:n, t, tok], r_q[r, 4 + h // 2, j0:j0 + n], r_q[r, h // 2, :],
                                               start=True, stop=True)
                    ins.then_inc(sr["s"], 1)
                    if h >= 1:
                        head_output(h - 1)
            pe.wait_ge(sr["in"], IN_R)
            for h in range(RH + 1):
                if h == 1:
                    head_output(RH - 1)
                if h < RH:
                    pe.wait_ge(sr["yc"], h + 1)
                    if h >= 4:
                        pe.wait_ge(sr["yd"], h - 3)
                    nc.tensor.matmul(ps[:, 4 + h % 4, tok], meanw[:, :], r_y[:, y_of(h), :], start=True,
                                     stop=True).then_inc(sr["mu"], 1)
                if h >= 1:
                    g = h - 1
                    pe.wait_ge(sr["ysq"], g + 1)
                    if g >= 4:
                        pe.wait_ge(sr["sdv"], g - 3)
                    if g == 0:
                        pe.wait_ge(sr["sd"], RH)
                    if g == 3:
                        pe.wait_ge(sr["yc"], RH)
                    nc.tensor.matmul(ps[:, g % 4, tok], meanw[:, :], r_ysq[:, g % 2, :], start=True,
                                     stop=True).then_inc(sr["var"], 1)
            pe.wait_ge(sr["sdv"], 8)
            pe.wait_ge(sr["yd"], 8)
            pe.wait_ge(sr["cl"], 2)
            gu = g0 + IN_R
            gr = gu + 4
            for c in range(2):
                slot_blocks(pe, gu + c, [ps[0:MQK, 4 * c + b, tok] for b in range(4)], (r_cqh, r_cql), widths=[MQK] * 4, tok=tok)
            for c in range(2):
                pe.wait_ge(sr["qc"], c + 1)
                for b in range(4):
                    ins = nc.tensor.matmul(ps[NOPE:MQK, 4 * c + b, tok], r_tab["m_rot"][NOPE:MQK, NOPE:MQK],
                                           r_qc[NOPE:MQK, 4 * c + b, :], start=True, stop=True)
                ins.then_inc(sr["qrot"], 1)
            pe.wait_ge(sr["qr"], 1)
            slot_blocks(pe, gu + 2, [ps[:, b, tok] for b in range(4)], (r_ckh, r_ckl), tok=tok)
            pe.wait_ge(sr["qr"], 2)
            pe.wait_ge(sr["zeros"], 1)
            s, nk = (gu + 3) % SLOTS, 2
            pe.wait_ge(w_lo, gu + 4)
            for t in range(3):
                o, cols = ps[:, 4 + t, :], slice(t * P, t * P + P)
                for k in range(nk):
                    w = slice(k * 512, k * 512 + 512)
                    nc.tensor.matmul(o, r_ckh[:, k, cols], whi[:, s, w], start=(k == 0), stop=False)
                    nc.tensor.matmul(o, r_ckl[:, k, cols], whi[:, s, w], start=False, stop=False)
                    ins = nc.tensor.matmul(o, r_ckh[:, k, cols], wlo[:, s, w], start=False, stop=(k == nk - 1))
            ins.then_inc(w_used, 1)
            pe.wait_ge(sr["kc"], 1)
            pe.wait_ge(sr["vm"], 1)

            def retention_block(f):
                g, c = gr + f // 2, (f % 2) * P
                s = g % SLOTS
                if f == 0:
                    pe.wait_ge(sr["yl"], 8)
                else:
                    pe.wait_ge(sr["gr"], f)
                pe.wait_ge(w_lo, g + 1)
                for k in range(KB):
                    w = slice(k * WIDE + c, k * WIDE + c + P)
                    nc.tensor.matmul(ps[:, 7, tok], whi[:, s, w], r_yh[:, k, :], start=(k == 0), stop=False)
                    nc.tensor.matmul(ps[:, 7, tok], whi[:, s, w], r_yl[:, k, :], start=False, stop=False)
                    ins = nc.tensor.matmul(ps[:, 7, tok], wlo[:, s, w], r_yh[:, k, :], start=False, stop=(k == KB - 1))
                ins.then_inc(w_used if f % 2 else sr["rb"], 1)

            for h in range(MH + 2):
                if h < MH:
                    if h >= 2:
                        pe.wait_ge(sr["ptc"], h - 1)
                        pe.wait_ge(sr["pta"], h - 1)
                    for t, (i0, n) in enumerate(TILES):
                        ins = nc.tensor.matmul(ps[0:n, 3 * (h % 2) + t, tok], r_qc[0:MQK, h, i0:i0 + n], r_kc[0:MQK, h, :], start=True, stop=True)
                    ins.then_inc(sr["sm"], 1)
                    retention_block(h)
                if 1 <= h <= MH:
                    g = h - 1
                    pe.wait_ge(sr["p"], g + 1)
                    for t, (j0, nj) in enumerate(TILES):
                        for u, (i0, ni) in enumerate(TILES):
                            ins = nc.tensor.transpose(ps[0:nj, 3 * (g % 2) + t, i0:i0 + ni], r_p[0:ni, g % 2, u, j0:j0 + nj], ident[0:ni, 0:ni])
                    ins.then_inc(sr["pt"], 1)
                if h >= 2:
                    g = h - 2
                    pair, r = g // 2, slice(MDV * (g % 2), MDV * (g % 2) + MDV)
                    pe.wait_ge(sr["ptc"], g + 1)
                    pe.wait_ge(sr["pta"], g + 1)
                    if pair >= 1:
                        pe.wait_ge(sr["ol"], pair)
                    for t, (j0, nj) in enumerate(TILES):
                        ins = nc.tensor.matmul(ps[r, 6, tok], r_vm[0:nj, t, g * MDV:g * MDV + MDV],
                                               r_pt[0:nj, g % 2, t, :], start=(t == 0), stop=(t == 2))
                    ins.then_inc(sr["ov"], 1)
            pe.wait_ge(sr["ol"], 4)
            pe.wait_ge(sr["ex"], 8)
            gm = gr + 4
            for c in range(4):
                if c >= 2:
                    pe.wait_ge(sr["gm"], c - 1)
                slot_blocks(pe, gm + c, [ps[:, 2 * (c % 2) + b, tok] for b in range(2)], (r_oh, r_ol), tok=tok)
            out_pe(pe, "R", [8], (r_mh, r_ml), ready=(sr["ml"], 0, 2))

        def r_act(act, ahead):
            g0, tok = first_slot["R"], tok_of["R"]
            ahead.to(g0 + 3)
            root(act, "R")

            def head_copy(h):
                act.wait_ge(sr["o"], h + 1)
                nc.scalar.activation(r_y[:, y_of(h), :], ps[:, 3, tok], ACT.Copy).then_inc(sr["yc"], 1)

            act.wait_ge(sr["par"], 32)
            nc.scalar.activation(r_lg[:, :, :], r_par[:, :, :], ACT.Exp).then_inc(sr["wx"], 1)
            for m in range(IN_R):
                ahead.to(g0 + m + 3)
                if 5 <= m <= 8:
                    act.wait_ge(sr["vt"], m - 4)
                    f = slice(2 * (m - 5) * P, 2 * (m - 4) * P)
                    nc.scalar.activation(r_v[:, 0:2, f].rearrange("p t (b c) -> p b t c", b=2),
                                         ps[:, 6:8, 0:2 * P].rearrange("p b (t c) -> p b t c", t=2), ACT.Copy)
                    nc.scalar.activation(r_v[0:META, 2, f].rearrange("p (b c) -> p b c", b=2), ps[0:META, 6:8, 2 * P:3 * P],
                                         ACT.Copy).then_inc(sr["vc"], 1)
                if m == 12:
                    act.wait_ge(sr["in"], 11)
                    act.wait_ge(s_sum, 2 * norm_no["R"] + 2)
                    nc.scalar.activation(r_csq[:, :, :], r_c[:, :, :], ACT.Square).then_inc(sr["csq"], 1)
                if m == 14:
                    act.wait_ge(sr["csum"], 1)
                    for i, n in enumerate((Q_RANK, KV_RANK)):
                        ins = nc.scalar.activation(r_csd[:, i], ps[:, 6 + i, tok], ACT.Sqrt, scale=1.0 / n, bias=eps_t[:, 0:1])
                    ins.then_inc(sr["csd"], 1)
                if m >= 16:
                    if m >= 18:
                        head_copy(m - 18)
                    act.wait_ge(sr["w"], m - 15)
                    nc.scalar.activation(r_W[:, m % 2], r_W[:, m % 2], ACT.Exp).then_inc(sr["wx"], 1)
                if m >= 12:
                    act.wait_ge(sr["in"], m + 1)
                    n = m - 12 if m < 16 else (m - 16) % 4
                    dst = (r_srg if m < 16 else r_gr if m < 20 else r_gm)[:, 2 * n:2 * n + 2, :]
                    nc.scalar.activation(dst, r_t[:, m % 2], ACT.Silu if m < 16 else ACT.Sigmoid).then_inc(sr["act"], 1)
            head_copy(RH - 2)
            head_copy(RH - 1)
            act.wait_ge(sr["cn"], 2)
            act.wait_ge(sr["o"], RH)
            nc.scalar.activation(r_cqh[:, :, :], r_c[:, 0:3, :], ACT.Copy).then_inc(sr["ch"], 1)
            nc.scalar.activation(r_ckh[:, :, tok], r_c[:, 3:5, :], ACT.Copy).then_inc(sr["ch"], 1)
            for h in range(RH + 2):
                if h < RH:
                    act.wait_ge(sr["yd"], h + 1)
                    if h >= 2:
                        act.wait_ge(sr["var"], h - 1)
                    nc.scalar.activation(r_ysq[:, h % 2], r_y[:, y_of(h), :], ACT.Square).then_inc(sr["ysq"], 1)
                if 1 <= h <= RH:
                    g = h - 1
                    act.wait_ge(sr["var"], g + 1)
                    if g >= 2:
                        act.wait_ge(sr["rec"], g - 1)
                    nc.scalar.activation(r_sd[:, g % 2], ps[:, g % 4, tok], ACT.Sqrt, bias=eps_t[:, 1:2]).then_inc(sr["sdv"], 1)
                if h >= 2:
                    g = h - 2
                    act.wait_ge(sr["yn"], 2 * g + 2)
                    nc.scalar.activation(r_yh[:, g, :], r_y[:, y_of(g), :], ACT.Copy).then_inc(sr["yh"], 1)
            gu = g0 + IN_R
            gr = gu + 4
            ahead.to(gu + 4)
            for c in range(2):
                act.wait_ge(w_used, gu + 1 + c)
                nc.scalar.activation(r_qc[0:MQK, 4 * c:4 * c + 4, :], ps[0:MQK, 4 * c:4 * c + 4, tok], ACT.Copy).then_inc(sr["qc"], 1)
            act.wait_ge(w_used, gu + 4)
            for t, n in enumerate((P, P, META)):
                ins = nc.scalar.activation(r_vm[0:n, t, :], ps[0:n, 4 + t, :], ACT.Copy)
            ins.then_inc(sr["vm"], 1)
            gm = gr + 4
            ahead.to(gr + 2)
            for h in range(MH + 2):
                if h < MH:
                    act.wait_ge(sr["nm"], h + 1)
                    if h >= 2:
                        act.wait_ge(sr["pt"], h - 1)
                    for t, (i0, n) in enumerate(TILES):
                        ins = nc.scalar.activation(r_p[0:n, h % 2, t, :], ps[0:n, 3 * (h % 2) + t, tok], ACT.Exp, scale=MQK ** -0.5,
                                                   bias=r_st[0:n, 1, h, t:t + 1], accum_out=r_st[0:n, 2, h, t:t + 1])
                    ins.then_inc(sr["ex"], 1)
                if 1 <= h <= MH:
                    g = h - 1
                    act.wait_ge(sr["pt"], g + 1)
                    if g >= 2:
                        act.wait_ge(sr["ov"], g - 1)
                    nc.scalar.activation(r_pt[0:META, g % 2, 2, :], ps[0:META, 3 * (g % 2) + 2, tok],
                                         ACT.Copy).then_inc(sr["pta"], 1)
                if h >= 3 and h % 2 == 1:
                    pair = (h - 3) // 2
                    act.wait_ge(sr["ov"], 2 * pair + 2)
                    nc.scalar.activation(r_oh[:, pair, :], ps[:, 6, tok], ACT.Copy).then_inc(sr["oh"], 1)
                ahead.to(gr + 2 + min(h + 1, 8) // 2)
            for c in range(4):
                if c < 3:
                    ahead.to(gm + c + 3)
                act.wait_ge(sr["mx"], 8 + c + 1)
                nc.scalar.activation(r_mh[:, 2 * c:2 * c + 2, :], r_gm[:, 2 * c:2 * c + 2, :], ACT.Copy).then_inc(sr["mh"], 1)
            out_act(act, "R", next_of("R"), 1, ahead)

        def r_dve(dve, ahead):
            g0, tok = first_slot["R"], tok_of["R"]
            ahead.to(g0 + 3)
            reciprocal_root(dve, "R")
            dve.wait_ge(s_rstd, norm_no["R"] + 1)
            r2 = over_pair(rstd[:, :], [P, 2, TOK])
            dve.wait_ge(sr["tab"], 16 * len(TABLES_OF["R"]))
            dve.wait_ge(sr["wx"], 1)
            nc.vector.tensor_scalar(r_lg[:, 0, :], r_lg[:, 0, :], -1.0, None, ALU.mult).then_inc(sr["lg"], 1)
            n_rope = [0]

            def rope(src, rot, cos, sin, dst, tmp, s_done):
                nc.vector.tensor_tensor(tmp[0], src, cos, ALU.mult)
                nc.vector.tensor_tensor(tmp[1], rot, sin, ALU.mult).then_inc(sr["qrd"], 1)
                n_rope[0] += 1
                dve.wait_ge(sr["qrd"], n_rope[0])
                nc.vector.tensor_tensor(dst, tmp[0], tmp[1], ALU.add).then_inc(s_done, 1)

            def decay_exponents(h):
                dve.wait_ge(sr["e"], h + 1)
                if h >= 2:
                    dve.wait_ge(sr["sd"], h - 1)
                if h == 0:
                    dve.wait_ge(sr["cn"], 2)
                nc.vector.scalar_tensor_tensor(r_W[:, h % 2], r_tab["r_dist"][:, :, :], r_lg[:, 0, h:h + 1], r_e[:, :, :],
                                               ALU.mult, ALU.min).then_inc(sr["w"], 1)

            def decayed_scores(g):
                dve.wait_ge(sr["s"], g + 1)
                dve.wait_ge(sr["wx"], g + 2)
                if g >= 1:
                    dve.wait_ge(sr["o"], g)
                nc.vector.scalar_tensor_tensor(r_s[:, 0:2], ps[:, 0:2, tok], RDK ** -0.5, r_W[:, g % 2, 0:2], ALU.mult, ALU.mult)
                nc.vector.scalar_tensor_tensor(r_s[0:META, 2], ps[0:META, 2, tok], RDK ** -0.5, r_W[0:META, g % 2, 2],
                                               ALU.mult, ALU.mult).then_inc(sr["sd"], 1)

            cos2, sin2 = [over_pair(r_tab[n][:, :], [P, 2, TOK]) for n in ("r_cos", "r_sin")]
            for m in range(IN_R + 1):
                if m < IN_R:
                    ahead.to(g0 + m + 3)
                    b0, nb = in_bank(m), slots[g0 + m][4] // P
                    if m >= 16:
                        if m >= 17:
                            decayed_scores(m - 17)
                        decay_exponents(m - 16)
                    dve.wait_ge(w_used, g0 + m + 1)
                    src, r = ps[:, b0:b0 + nb, tok], r2 if nb == 2 else rstd[:, :].unsqueeze(1)
                    if 8 <= m <= 10:
                        c = (0, 2, 3)[m - 8]
                        nc.vector.tensor_tensor(r_c[:, c:c + nb, :], src, r, ALU.mult).then_inc(sr["in"], 1)
                    else:
                        if 6 <= m <= 7:
                            dve.wait_ge(sr["vt"], m - 5)
                        if m == 11 or m == 12:
                            dve.wait_ge(sr["vt"], 4)
                        if m == 13:
                            dve.wait_ge(sr["rope"], 5)
                        if m >= 14:
                            dve.wait_ge(sr["act"], m - 13)
                        nc.vector.tensor_tensor(r_t[:, m % 2, 0:nb], src, r, ALU.mult).then_inc(sr["in"], 1)
                if 1 <= m <= 4:
                    dve.wait_ge(sr["rot"], m)
                    rope(r_t[:, (m - 1) % 2], ps[:, 6:8, tok], cos2, sin2, r_q[:, 2 * m - 2:2 * m, :],
                         (r_t2[:, 0], r_t2[:, 1]), sr["rope"])
                if m == 12:
                    dve.wait_ge(sr["rot"], 5)
                    rope(r_t[0:ROPE, 1, 0, :], ps[0:ROPE, 6, tok], r_tab["m_cos"][0:ROPE, :], r_tab["m_sin"][0:ROPE, :],
                         r_kr[0:ROPE, :], (r_t2[0:ROPE, 0, 0], r_t2[0:ROPE, 1, 0]), sr["rope"])
                if m == 14:
                    dve.wait_ge(sr["csd"], 1)
                    for i in range(2):
                        ins = nc.vector.reciprocal(r_csd[:, i], r_csd[:, i])
                    ins.then_inc(sr["cr"], 1)
                if m == 15:
                    dve.wait_ge(sr["cr"], 1)
                    for i, (k0, n, nm) in enumerate(((0, 3, "mla_q_norm_w_2"), (3, 2, "mla_kv_norm_w_2"))):
                        for b in range(n):
                            w = VEC_ROWS[nm] + b
                            ins = nc.vector.scalar_tensor_tensor(r_c[:, k0 + b, :], r_c[:, k0 + b, :], vec[:, w:w + 1],
                                                                 r_csd[:, i], ALU.mult, ALU.mult)
                        ins.then_inc(sr["cn"], 1)
            decayed_scores(RH - 1)
            for h in range(RH + 3):
                if h < RH:
                    dve.wait_ge(sr["mu"], h + 1)
                    nc.vector.tensor_tensor(r_y[:, y_of(h), :], r_y[:, y_of(h), :], ps[:, 4 + h % 4, tok], ALU.subtract).then_inc(sr["yd"], 1)
                if 1 <= h <= RH:
                    g = h - 1
                    w = VEC_ROWS["ret_gn_w_2"] + g
                    dve.wait_ge(sr["sdv"], g + 1)
                    nc.vector.reciprocal(r_sd[:, g % 2], r_sd[:, g % 2]).then_inc(sr["rec"], 1)
                    dve.wait_ge(sr["rec"], g + 1)
                    nc.vector.scalar_tensor_tensor(r_y[:, y_of(g), :], r_y[:, y_of(g), :], vec[:, w:w + 1], r_sd[:, g % 2], ALU.mult,
                                                   ALU.mult).then_inc(sr["yn"], 1)
                    dve.wait_ge(sr["yn"], 2 * g + 1)
                    nc.vector.tensor_tensor(r_y[:, y_of(g), :], r_y[:, y_of(g), :], r_srg[:, g, :], ALU.mult).then_inc(sr["yn"], 1)
                if h == 2:
                    dve.wait_ge(sr["ch"], 1)
                    nc.vector.tensor_tensor(r_cql[:, :, :], r_c[:, 0:3, :], r_cqh[:, :, :].bitcast(F32), ALU.subtract).then_inc(sr["cl"], 1)
                    dve.wait_ge(sr["ch"], 2)
                    nc.vector.tensor_tensor(r_ckl[:, :, tok], r_c[:, 3:5, :], r_ckh[:, :, tok].bitcast(F32), ALU.subtract).then_inc(sr["cl"], 1)
                if h >= 3:
                    g = h - 3
                    dve.wait_ge(sr["yh"], g + 1)
                    nc.vector.tensor_tensor(r_yl[:, g, :], r_y[:, y_of(g), :], r_yh[:, g, :].bitcast(F32), ALU.subtract).then_inc(sr["yl"], 1)
            gu = g0 + IN_R
            gr = gu + 4
            ahead.to(gu + 4)
            dve.wait_ge(sr["yl"], 8)
            kr = r_kr[0:ROPE, :].unsqueeze(1).broadcast_to([ROPE, MH, TOK])
            nc.vector.tensor_copy(r_kc[NOPE:MQK, :, :], kr)
            for c in range(2):
                dve.wait_ge(sr["qrot"], c + 1)
                if c:
                    dve.wait_ge(sr["qr"], 1)
                rr = slice(NOPE, MQK)
                cs, sn = [r_tab[n][rr, :].unsqueeze(1).broadcast_to([ROPE, 4, TOK]) for n in ("m_cos", "m_sin")]
                q4 = r_qc[rr, 4 * c:4 * c + 4, :]
                rope(q4, ps[rr, 4 * c:4 * c + 4, tok], cs, sn, q4, (r_rt[rr, 0], r_rt[rr, 1]), sr["qr"])
            dve.wait_ge(w_used, gu + 3)
            kv = r_kc[0:NOPE, :, :].rearrange("p (b e) t -> p b e t", e=2)
            for e in range(2):
                ins = nc.vector.tensor_copy(kv[:, :, e, :], ps[NOPE * e:NOPE * e + NOPE, 0:4, tok])
            ins.then_inc(sr["kc"], 1)
            gm = gr + 4
            ahead.to(gr + 2)
            sc = -(MQK ** -0.5)
            for h in range(MH + 3):
                if 1 <= h <= MH:
                    f = h - 1
                    if f % 2:
                        dve.wait_ge(w_used, gr + f // 2 + 1)
                    else:
                        dve.wait_ge(sr["rb"], f // 2 + 1)
                    nc.vector.tensor_tensor(r_gr[:, f, :], ps[:, 7, tok], r_gr[:, f, :], ALU.mult).then_inc(sr["gr"], 1)
                if h < MH:
                    dve.wait_ge(sr["sm"], h + 1)
                    b0 = 3 * (h % 2)
                    nc.vector.tensor_reduce(r_st[:, 0, h, 0:2], ps[:, b0:b0 + 2, tok], AX.X, ALU.max)
                    nc.vector.tensor_reduce(r_st[0:META, 0, h, 2:3], ps[0:META, b0 + 2, tok], AX.X, ALU.max).then_inc(sr["mx"], 1)
                    dve.wait_ge(sr["mx"], h + 1)
                    nc.vector.tensor_scalar(r_st[:, 1, h, 0:2], r_st[:, 0, h, 0:2], sc, None, ALU.mult)
                    nc.vector.tensor_scalar(r_st[0:META, 1, h, 2:3], r_st[0:META, 0, h, 2:3], sc, None, ALU.mult).then_inc(sr["nm"], 1)
                if h >= 4 and h % 2 == 0:
                    pair = h // 2 - 2
                    dve.wait_ge(sr["oh"], pair + 1)
                    nc.vector.tensor_tensor(r_ol[:, pair, :], ps[:, 6, tok], r_oh[:, pair, :].bitcast(F32),
                                            ALU.subtract).then_inc(sr["ol"], 1)
                if 1 <= h <= MH:
                    g = h - 1
                    dve.wait_ge(sr["ex"], g + 1)
                    nc.vector.reciprocal(r_st[:, 3, g, 0:2], r_st[:, 2, g, 0:2])
                    nc.vector.reciprocal(r_st[0:META, 3, g, 2:3], r_st[0:META, 2, g, 2:3]).then_inc(sr["rs"], 1)
                    dve.wait_ge(sr["rs"], g + 1)
                    for t, (i0, n) in enumerate(TILES):
                        ins = nc.vector.tensor_scalar(r_p[0:n, g % 2, t], r_p[0:n, g % 2, t], r_st[0:n, 3, g, t:t + 1], None, ALU.mult)
                    ins.then_inc(sr["p"], 1)
                    dve.wait_ge(sr["pt"], g + 1)
                    if g >= 2:
                        dve.wait_ge(sr["ov"], g - 1)
                    nc.vector.tensor_copy(r_pt[:, g % 2, 0:2], ps[:, 3 * (g % 2):3 * (g % 2) + 2, tok]).then_inc(sr["ptc"], 1)
                ahead.to(gr + 2 + min(h + 1, 8) // 2)
            for c in range(4):
                if c < 3:
                    ahead.to(gm + c + 3)
                s2 = slice(2 * c, 2 * c + 2)
                dve.wait_ge(w_used, gm + c + 1)
                nc.vector.tensor_tensor(r_gm[:, s2, :], ps[:, 2 * (c % 2):2 * (c % 2) + 2, tok], r_gm[:, s2, :],
                                        ALU.mult).then_inc(sr["gm"], 1)
                dve.wait_ge(sr["gm"], c + 1)
                nc.vector.tensor_tensor(r_gm[:, s2, :], r_gm[:, s2, :], r_gr[:, s2, :], ALU.add).then_inc(sr["mx"], 1)
                dve.wait_ge(sr["mh"], c + 1)
                nc.vector.tensor_tensor(r_ml[:, s2, :], r_gm[:, s2, :], r_mh[:, s2, :].bitcast(F32), ALU.subtract).then_inc(sr["ml"], 1)
            out_dve(dve, "R", next_of("R"), 1, 1.0, ahead)

        mixer_load["R"], mixer_pool["R"], mixer_act["R"], mixer_dve["R"], mixer_pe["R"] = r_load, r_pool, r_act, r_dve, r_pe

        block = ctx.enter_context(nc.Block())

        @block.sync
        def _(sp):
            for st in stages:
                if st[0] == "F":
                    ffn_load(sp, st)
                elif st in mixer_load:
                    mixer_load[st](sp)
            last_store(sp)

        @block.gpsimd
        def _(pool):
            other_loads(pool)
            for st in stages:
                fold_squares(pool, st)
                if st in mixer_pool:
                    mixer_pool[st](pool)
            fold_squares(pool, "end")
            pool.wait_ge(l_ones, 48)

        @block.scalar
        def _(act):
            ahead = Ahead(act, round_slot)
            first_loads(act)
            first_act(act, ahead)
            for st in stages:
                if st[0] == "F":
                    ffn_act(act, st, ahead)
                elif st == "N":
                    norm_act(act)
                else:
                    mixer_act[st](act, ahead)
            last_act(act)

        @block.vector
        def _(dve):
            ahead = Ahead(dve, rest_slot)
            first_dve(dve, ahead)
            for st in stages:
                if st[0] == "F":
                    ffn_dve(dve, st, ahead)
                elif st == "N":
                    norm_dve(dve)
                else:
                    mixer_dve[st](dve, ahead)
            last_dve(dve)

        @block.tensor
        def _(pe):
            first_pe(pe)
            for st in stages:
                if st[0] == "F":
                    ffn_pe(pe, st)
                elif st == "N":
                    norm_pe(pe)
                else:
                    mixer_pe[st](pe)
            last_pe(pe)


def kernel(**inputs):
    import concourse.bacc as bacc
    from concourse.bass_utils import run_bass_kernel_spmd

    f = lambda name: np.ascontiguousarray(np.asarray(inputs[name]))
    columns = lambda a: a.reshape(-1, P).T
    tokens = np.concatenate([f("meta_tokens_2"), f("x")[0]], 0)
    arrays = {"x": tokens.T.reshape(KB, P, TOK).transpose(1, 0, 2)}
    vectors = {"a_w_conv": columns(f("a_w_conv"))}
    for layer in range(2):
        for name in ("ffn1_w_gu", "ffn1_w_down", "ffn2_w_gu", "ffn2_w_down"):
            arrays[f"{name}_{layer}"] = f(name)[layer]
        for name in ("ffn1_norm", "mix_norm", "ffn2_norm"):
            vectors[f"{name}_{layer}"] = columns(f(name)[layer])
    for name in ("a_w_in", "a_w_out", "b_w_in", "b_w_out", "w_in_2", "w_ret_out_2", "w_uq_2", "w_uk_2", "w_uv_2",
                 "w_mla_out_2", "w_o_2", "w_ffn_gate_2", "w_ffn_up_2", "w_ffn_down_2"):
        arrays[name] = f(name)[0]
    for name in ("final_norm", "norm_mix_w_2", "norm_ffn_w_2", "norm_final_w_2", "ret_gn_w_2", "mla_q_norm_w_2",
                 "mla_kv_norm_w_2", "a_out_norm", "b_b_in", "b_b_out"):
        vectors[name] = columns(f(name))
    arrays["vectors"] = np.concatenate([vectors[name] for name in VEC_ROWS] + [vectors["a_w_conv"]], 1)
    for name in ("a_A_log", "a_dt_bias", "b_sinks", "ret_decay_fwd_2", "ret_decay_bwd_2"):
        arrays[name] = f(name).reshape(1, -1)
    arrays.update(constants())
    arrays = {k: np.ascontiguousarray(v) for k, v in arrays.items()}

    nc = bacc.Bacc("TRN2", target_bir_lowering=False, num_devices=1)
    dram = {k: nc.dram_tensor(f"in_{k}", v.shape, mybir.dt.from_np(v.dtype), kind="ExternalInput").ap()
            for k, v in arrays.items()}
    out = nc.dram_tensor("out_y", (P, KB, SEQ), F32, kind="ExternalOutput").ap()
    build(nc, dram, out)
    r = run_bass_kernel_spmd(nc, [{f"in_{k}": v for k, v in arrays.items()}], core_ids=[0])
    return np.ascontiguousarray(r.results[0]["out_y"].transpose(2, 1, 0).reshape(1, SEQ, D))
```
